# Optimizing a Trainium2 kernel written in Bass

```python
import math
import jax, jax.numpy as jnp
from jax import lax
import numpy as np

D_MODEL = 1024
BATCH = 1
SEQ = 256
DEPTH = 2

N_EVEN = (DEPTH + 1) // 2
N_ODD = DEPTH // 2
EPS = 1e-6

CONF_WIDTH = D_MODEL // 2
CONF_KERNEL = 31
LRU_WIDTH = D_MODEL // 2
LRU_HEADS = 8
LRU_HEAD_DIM = LRU_WIDTH // LRU_HEADS
LRU_CONV = 4
LRU_C = 8.0
AB_IN = 2 * CONF_WIDTH + 2 * LRU_WIDTH
AB_OUT = CONF_WIDTH + LRU_WIDTH
ML_HEADS = 8
ML_V_DIM = D_MODEL
ML_HEAD_V = ML_V_DIM // ML_HEADS
ML_HEAD_QK = ML_HEAD_V // 2
ML_QK_DIM = ML_HEADS * ML_HEAD_QK
ML_CHUNK = 64
ML_IN = 2 * ML_QK_DIM + 2 * ML_V_DIM + 2 * ML_HEADS
D_FF = int(math.ceil(8 * D_MODEL / 3 / 256)) * 256


def _rmsnorm(x, g):
    xf = x.astype(jnp.float32)
    y = xf * lax.rsqrt(jnp.mean(xf * xf, axis=-1, keepdims=True) + EPS)
    return (y * g.astype(jnp.float32)).astype(x.dtype)

def _layernorm(x, g, b):
    xf = x.astype(jnp.float32)
    mu = jnp.mean(xf, axis=-1, keepdims=True)
    var = jnp.mean(jnp.square(xf - mu), axis=-1, keepdims=True)
    y = (xf - mu) * lax.rsqrt(var + EPS)
    return (y * g.astype(jnp.float32) + b.astype(jnp.float32)).astype(x.dtype)

def _causal_dwconv(x, w, b):
    k = w.shape[0]
    c = x.shape[-1]
    y = lax.conv_general_dilated(
        x, w[:, None, :].astype(x.dtype), window_strides=(1,), padding=[(k - 1, 0)],
        dimension_numbers=('NWC', 'WIO', 'NWC'), feature_group_count=c)
    return y + b

def _conformer_conv(u, conv_w, conv_b, ln_g, ln_b):
    val, gate = jnp.split(u, 2, axis=-1)
    y = val * jax.nn.sigmoid(gate)
    y = _causal_dwconv(y, conv_w, conv_b)
    return jax.nn.silu(_layernorm(y, ln_g, ln_b))

def _lru_combine(left, right):
    a_l, b_l = left
    a_r, b_r = right
    return a_l * a_r, a_r * b_l + b_r

def _rglru_block(u, conv_w, conv_b, w_a, b_a, w_x, b_x, lam):
    bsz, seq, _ = u.shape
    gate_in, rec_in = jnp.split(u, 2, axis=-1)
    xr = _causal_dwconv(rec_in, conv_w, conv_b)
    xh = xr.reshape(bsz, seq, LRU_HEADS, LRU_HEAD_DIM)
    r = jax.nn.sigmoid(jnp.einsum('bshd,hde->bshe', xh, w_a) + b_a)
    i = jax.nn.sigmoid(jnp.einsum('bshd,hde->bshe', xh, w_x) + b_x)
    log_base = -jax.nn.softplus(-lam.astype(jnp.float32)).reshape(LRU_HEADS, LRU_HEAD_DIM)
    log_a = LRU_C * log_base * r.astype(jnp.float32)
    a = jnp.exp(log_a)
    gated_x = jnp.sqrt(-jnp.expm1(2.0 * log_a)) * (i * xh).astype(jnp.float32)
    _, h = lax.associative_scan(_lru_combine, (a, gated_x), axis=1)
    h = h.reshape(bsz, seq, LRU_WIDTH).astype(u.dtype)
    return h * jax.nn.gelu(gate_in)

def _ab_mixer(xn, w_in, b_in, conf_conv_w, conf_conv_b, conf_ln_g, conf_ln_b,
              lru_conv_w, lru_conv_b, lru_w_a, lru_b_a, lru_w_x, lru_b_x, lru_lambda, w_out):
    u = jnp.einsum('bsd,de->bse', xn, w_in) + b_in
    u_conf, u_lru = jnp.split(u, [2 * CONF_WIDTH], axis=-1)
    y_a = _conformer_conv(u_conf, conf_conv_w, conf_conv_b, conf_ln_g, conf_ln_b)
    y_b = _rglru_block(u_lru, lru_conv_w, lru_conv_b, lru_w_a, lru_b_a, lru_w_x, lru_b_x, lru_lambda)
    y = jnp.concatenate([y_a, y_b], axis=-1)
    return jnp.einsum('bse,ed->bsd', y, w_out)

def _mlstm_chunk_step(carry, inp):
    c_state, n_state, m_state = carry
    qc, kc, vc, ic, lfc = inp
    L = qc.shape[2]
    causal = jnp.tril(jnp.ones((L, L), dtype=bool))
    b = jnp.cumsum(lfc, axis=-1)
    log_d = b[..., :, None] - b[..., None, :] + ic[..., None, :]
    log_d = jnp.where(causal, log_d, -jnp.inf)
    log_inter = b + m_state[..., None]
    m_row = jnp.maximum(log_inter, jnp.max(log_d, axis=-1))
    d_w = jnp.exp(log_d - m_row[..., None])
    inter_w = jnp.exp(log_inter - m_row)
    scores = jnp.einsum('bhjd,bhsd->bhjs', qc, kc) * d_w
    num = jnp.einsum('bhjs,bhsv->bhjv', scores, vc) + inter_w[..., None] * jnp.einsum('bhjd,bhdv->bhjv', qc, c_state)
    den = jnp.sum(scores, axis=-1) + inter_w * jnp.einsum('bhjd,bhd->bhj', qc, n_state)
    h = num / jnp.maximum(jnp.abs(den), jnp.exp(-m_row))[..., None]
    b_last = b[..., -1]
    log_w = b_last[..., None] - b + ic
    m_new = jnp.maximum(b_last + m_state, jnp.max(log_w, axis=-1))
    w_s = jnp.exp(log_w - m_new[..., None])
    decay = jnp.exp(b_last + m_state - m_new)
    c_new = decay[..., None, None] * c_state + jnp.einsum('bhsd,bhsv->bhdv', w_s[..., None] * kc, vc)
    n_new = decay[..., None] * n_state + jnp.einsum('bhs,bhsd->bhd', w_s, kc)
    return (c_new, n_new, m_new), h

def _mlstm_mixer(xn, w_in, b_in, head_g, w_out):
    bsz, seq, _ = xn.shape
    nc = seq // ML_CHUNK
    u = jnp.einsum('bsd,de->bse', xn, w_in) + b_in
    q, k, v, o, ig, fg = jnp.split(
        u, [ML_QK_DIM, 2 * ML_QK_DIM, 2 * ML_QK_DIM + ML_V_DIM,
            2 * ML_QK_DIM + 2 * ML_V_DIM, 2 * ML_QK_DIM + 2 * ML_V_DIM + ML_HEADS], axis=-1)
    f32 = jnp.float32

    def to_chunks(t, d):
        return t.astype(f32).reshape(bsz, nc, ML_CHUNK, ML_HEADS, d).transpose(1, 0, 3, 2, 4)

    def gate_chunks(t):
        return t.astype(f32).reshape(bsz, nc, ML_CHUNK, ML_HEADS).transpose(1, 0, 3, 2)

    qc = to_chunks(q, ML_HEAD_QK)
    kc = to_chunks(k, ML_HEAD_QK) * (ML_HEAD_QK ** -0.5)
    vc = to_chunks(v, ML_HEAD_V)
    ic = gate_chunks(ig)
    lfc = gate_chunks(jax.nn.log_sigmoid(fg))
    init = (jnp.zeros((bsz, ML_HEADS, ML_HEAD_QK, ML_HEAD_V), f32),
            jnp.zeros((bsz, ML_HEADS, ML_HEAD_QK), f32),
            jnp.zeros((bsz, ML_HEADS), f32))
    _, h = lax.scan(_mlstm_chunk_step, init, (qc, kc, vc, ic, lfc))
    h = h.transpose(1, 0, 3, 2, 4).reshape(bsz, seq, ML_HEADS, ML_HEAD_V)
    h = h * lax.rsqrt(jnp.mean(h * h, axis=-1, keepdims=True) + EPS)
    h = (h.reshape(bsz, seq, ML_V_DIM) * head_g.astype(f32)).astype(xn.dtype)
    h = jax.nn.sigmoid(o) * h
    return jnp.einsum('bse,ed->bsd', h, w_out)

def _swiglu(xn, w_gate, w_up, w_down):
    g = jnp.einsum('bsd,df->bsf', xn, w_gate)
    up = jnp.einsum('bsd,df->bsf', xn, w_up)
    return jnp.einsum('bsf,fd->bsd', jax.nn.silu(g) * up, w_down)

def first_inputs(seed: int = 0) -> dict:
    key = jax.random.key(seed)
    ks = iter(jax.random.split(key, 40))

    def nrm(shape, scale):
        return jax.random.normal(next(ks), shape, jnp.float32) * scale

    def gain(shape):
        return 1.0 + nrm(shape, 0.05)

    lam_u = jax.random.uniform(next(ks), (N_EVEN, LRU_WIDTH), jnp.float32, minval=0.9, maxval=0.999)
    lam_base = lam_u ** (1.0 / LRU_C)
    lru_lambda = jnp.log(lam_base) - jnp.log1p(-lam_base)

    ml_b_in = nrm((N_ODD, ML_IN), 0.02)
    f_bias = jnp.linspace(3.0, 6.0, ML_HEADS, dtype=jnp.float32) + nrm((N_ODD, ML_HEADS), 0.1)
    ml_b_in = ml_b_in.at[:, ML_IN - ML_HEADS:].set(f_bias)

    return {
        'x': nrm((BATCH, SEQ, D_MODEL), 1.0),
        'pre_mix_g': gain((DEPTH, D_MODEL)),
        'post_mix_g': gain((DEPTH, D_MODEL)),
        'pre_ffn_g': gain((DEPTH, D_MODEL)),
        'post_ffn_g': gain((DEPTH, D_MODEL)),
        'ab_w_in': nrm((N_EVEN, D_MODEL, AB_IN), D_MODEL ** -0.5),
        'ab_b_in': nrm((N_EVEN, AB_IN), 0.02),
        'conf_conv_w': nrm((N_EVEN, CONF_KERNEL, CONF_WIDTH), CONF_KERNEL ** -0.5),
        'conf_conv_b': nrm((N_EVEN, CONF_WIDTH), 0.02),
        'conf_ln_g': gain((N_EVEN, CONF_WIDTH)),
        'conf_ln_b': nrm((N_EVEN, CONF_WIDTH), 0.02),
        'lru_conv_w': nrm((N_EVEN, LRU_CONV, LRU_WIDTH), LRU_CONV ** -0.5),
        'lru_conv_b': nrm((N_EVEN, LRU_WIDTH), 0.02),
        'lru_w_a': nrm((N_EVEN, LRU_HEADS, LRU_HEAD_DIM, LRU_HEAD_DIM), LRU_HEAD_DIM ** -0.5),
        'lru_b_a': nrm((N_EVEN, LRU_HEADS, LRU_HEAD_DIM), 0.02),
        'lru_w_x': nrm((N_EVEN, LRU_HEADS, LRU_HEAD_DIM, LRU_HEAD_DIM), LRU_HEAD_DIM ** -0.5),
        'lru_b_x': nrm((N_EVEN, LRU_HEADS, LRU_HEAD_DIM), 0.02),
        'lru_lambda': lru_lambda,
        'ab_w_out': nrm((N_EVEN, AB_OUT, D_MODEL), AB_OUT ** -0.5),
        'ml_w_in': nrm((N_ODD, D_MODEL, ML_IN), D_MODEL ** -0.5),
        'ml_b_in': ml_b_in,
        'ml_head_g': gain((N_ODD, ML_V_DIM)),
        'ml_w_out': nrm((N_ODD, ML_V_DIM, D_MODEL), ML_V_DIM ** -0.5),
        'ffn_w_gate': nrm((DEPTH, D_MODEL, D_FF), D_MODEL ** -0.5),
        'ffn_w_up': nrm((DEPTH, D_MODEL, D_FF), D_MODEL ** -0.5),
        'ffn_w_down': nrm((DEPTH, D_FF, D_MODEL), D_FF ** -0.5),
    }

def first_block(x, pre_mix_g, post_mix_g, pre_ffn_g, post_ffn_g,
              ab_w_in, ab_b_in, conf_conv_w, conf_conv_b, conf_ln_g, conf_ln_b,
              lru_conv_w, lru_conv_b, lru_w_a, lru_b_a, lru_w_x, lru_b_x, lru_lambda, ab_w_out,
              ml_w_in, ml_b_in, ml_head_g, ml_w_out,
              ffn_w_gate, ffn_w_up, ffn_w_down):
    for layer in range(DEPTH):
        j = layer // 2
        h = _rmsnorm(x, pre_mix_g[layer])
        if layer % 2 == 0:
            h = _ab_mixer(h, ab_w_in[j], ab_b_in[j], conf_conv_w[j], conf_conv_b[j],
                          conf_ln_g[j], conf_ln_b[j], lru_conv_w[j], lru_conv_b[j],
                          lru_w_a[j], lru_b_a[j], lru_w_x[j], lru_b_x[j], lru_lambda[j], ab_w_out[j])
        else:
            h = _mlstm_mixer(h, ml_w_in[j], ml_b_in[j], ml_head_g[j], ml_w_out[j])
        x = x + _rmsnorm(h, post_mix_g[layer])
        h = _swiglu(_rmsnorm(x, pre_ffn_g[layer]), ffn_w_gate[layer], ffn_w_up[layer], ffn_w_down[layer])
        x = x + _rmsnorm(h, post_ffn_g[layer])
    return x


GRID_W = 64
CTX_LEN = 256
N_Q_HEADS = 8
N_KV_HEADS = 2
GQA_GROUP = N_Q_HEADS // N_KV_HEADS
HEAD_DIM = 64
WINDOW = 128
ATT_BLOCK = 128
ROPE_BASE = 10000.0
Q_DIM = N_Q_HEADS * HEAD_DIM
KV_DIM = N_KV_HEADS * HEAD_DIM
SG_GROUPS = 8
SG_HEAD = 64
SG_WIDTH = SG_GROUPS * SG_HEAD
SG_CHUNK = 128
EVEN_IN = Q_DIM + 2 * KV_DIM + 2 * SG_WIDTH
EVEN_MIX = Q_DIM + SG_WIDTH
CONV_WIDTH = D_MODEL
CONV_K = 3
N_GROUPS = 4
EXPERTS_PER_GROUP = 8
N_EXPERTS = N_GROUPS * EXPERTS_PER_GROUP
TOP_K_IN_GROUP = 2
EXPERT_HIDDEN = D_MODEL // 2
MOE_BLOCK = 128
N_EVEN_2 = (DEPTH + 1) // 2
N_ODD_2 = DEPTH // 2
NEG_INF = -1e30


def rms_norm(x, g):
    xf = x.astype(jnp.float32)
    y = xf * lax.rsqrt(jnp.mean(xf * xf, axis=-1, keepdims=True) + EPS)
    return (y * g.astype(jnp.float32)).astype(x.dtype)

def layer_norm(x, g):
    xf = x.astype(jnp.float32)
    mu = jnp.mean(xf, axis=-1, keepdims=True)
    xc = xf - mu
    y = xc * lax.rsqrt(jnp.mean(xc * xc, axis=-1, keepdims=True) + EPS)
    return (y * g.astype(jnp.float32)).astype(x.dtype)

def modulate(h, shift, scale):
    return h * (1 + scale) + shift

def axial_rope_tables(rows, dtype):
    quarter = HEAD_DIM // 4
    row_ids = jnp.repeat(jnp.arange(rows, dtype=jnp.float32), GRID_W)
    col_ids = jnp.tile(jnp.arange(GRID_W, dtype=jnp.float32), rows)
    inv = ROPE_BASE ** (-jnp.arange(quarter, dtype=jnp.float32) / quarter)
    ang_r = row_ids[:, None] * inv
    ang_c = col_ids[:, None] * inv
    return (jnp.cos(ang_r)[:, None, :].astype(dtype), jnp.sin(ang_r)[:, None, :].astype(dtype),
            jnp.cos(ang_c)[:, None, :].astype(dtype), jnp.sin(ang_c)[:, None, :].astype(dtype))

def apply_axial_rope(t, rope):
    cos_r, sin_r, cos_c, sin_c = rope
    half = HEAD_DIM // 2
    quarter = HEAD_DIM // 4

    def rot(u, cos, sin):
        u1, u2 = u[..., :quarter], u[..., quarter:]
        return jnp.concatenate([u1 * cos - u2 * sin, u2 * cos + u1 * sin], axis=-1)

    return jnp.concatenate([rot(t[..., :half], cos_r, sin_r), rot(t[..., half:], cos_c, sin_c)], axis=-1)

def windowed_attention(q, k, v, kc, vc, sink):
    b, s = q.shape[:2]
    nb = s // ATT_BLOCK
    scale = HEAD_DIM ** -0.5
    f32 = jnp.float32
    qb = q.reshape(b, nb, ATT_BLOCK, N_KV_HEADS, GQA_GROUP, HEAD_DIM)

    def band(t):
        tp = jnp.pad(t, ((0, 0), (ATT_BLOCK, ATT_BLOCK), (0, 0), (0, 0)))
        tp = tp.reshape(b, nb + 2, ATT_BLOCK, N_KV_HEADS, HEAD_DIM)
        return jnp.concatenate([tp[:, :-2], tp[:, 1:-1], tp[:, 2:]], axis=2)

    kb, vb = band(k), band(v)
    s_loc = jnp.einsum('bnqhgd,bnkhd->bnhgqk', qb, kb, preferred_element_type=f32) * scale
    s_ctx = jnp.einsum('bnqhgd,bchd->bnhgqc', qb, kc, preferred_element_type=f32) * scale
    qi = jnp.arange(ATT_BLOCK)[:, None]
    kj = jnp.arange(3 * ATT_BLOCK)[None, :]
    in_win = jnp.abs(kj - qi - ATT_BLOCK) <= WINDOW
    kpos = (jnp.arange(nb)[:, None] - 1) * ATT_BLOCK + jnp.arange(3 * ATT_BLOCK)[None, :]
    mask = in_win[None] & ((kpos >= 0) & (kpos < s))[:, None, :]
    s_loc = jnp.where(mask[None, :, None, None], s_loc, NEG_INF)
    sink_l = jnp.broadcast_to(sink.astype(f32).reshape(1, 1, N_KV_HEADS, GQA_GROUP, 1, 1), s_ctx.shape[:-1] + (1,))
    p = jax.nn.softmax(jnp.concatenate([sink_l, s_ctx, s_loc], axis=-1), axis=-1)
    n_ctx = kc.shape[1]
    p_ctx = p[..., 1:1 + n_ctx].astype(vc.dtype)
    p_loc = p[..., 1 + n_ctx:].astype(vb.dtype)
    o = (jnp.einsum('bnhgqc,bchd->bnqhgd', p_ctx, vc)
         + jnp.einsum('bnhgqk,bnkhd->bnqhgd', p_loc, vb))
    return o.reshape(b, s, Q_DIM)

def context_attention(qc, kc, vc, sink):
    b, n = qc.shape[:2]
    f32 = jnp.float32
    qh = qc.reshape(b, n, N_KV_HEADS, GQA_GROUP, HEAD_DIM)
    sc = jnp.einsum('bqhgd,bkhd->bhgqk', qh, kc, preferred_element_type=f32) * (HEAD_DIM ** -0.5)
    sink_c = jnp.broadcast_to(sink.astype(f32).reshape(1, N_KV_HEADS, GQA_GROUP, 1, 1), sc.shape[:-1] + (1,))
    p = jax.nn.softmax(jnp.concatenate([sink_c, sc], axis=-1), axis=-1)
    o = jnp.einsum('bhgqk,bkhd->bqhgd', p[..., 1:].astype(vc.dtype), vc)
    return o.reshape(b, n, Q_DIM)

def spatial_gating(u, z, g_sgu, w_sp, b_sp):
    b, n = u.shape[:2]
    u = jax.nn.gelu(u, approximate=False)
    z = layer_norm(jax.nn.gelu(z, approximate=False), g_sgu)
    zc = z.reshape(b, n // SG_CHUNK, SG_CHUNK, SG_GROUPS, SG_HEAD)
    sgate = jnp.einsum('hij,bnjhc->bnihc', w_sp, zc) + b_sp.T[:, :, None]
    return (u.reshape(zc.shape) * sgate).reshape(b, n, SG_WIDTH)

def even_mixer(h, hc, w_in, sink, g_sgu, w_sp, b_sp, w_out, rope, need_ctx):
    b, s, _ = h.shape
    n_ctx = hc.shape[1]
    q, k, v, u, z = jnp.split(h @ w_in, [Q_DIM, Q_DIM + KV_DIM, Q_DIM + 2 * KV_DIM, Q_DIM + 2 * KV_DIM + SG_WIDTH], axis=-1)
    q = apply_axial_rope(q.reshape(b, s, N_Q_HEADS, HEAD_DIM), rope)
    k = apply_axial_rope(k.reshape(b, s, N_KV_HEADS, HEAD_DIM), rope)
    v = v.reshape(b, s, N_KV_HEADS, HEAD_DIM)
    kc, vc = jnp.split(hc @ w_in[:, Q_DIM:Q_DIM + 2 * KV_DIM], 2, axis=-1)
    kc = kc.reshape(b, n_ctx, N_KV_HEADS, HEAD_DIM)
    vc = vc.reshape(b, n_ctx, N_KV_HEADS, HEAD_DIM)
    att = windowed_attention(q, k, v, kc, vc, sink)
    sg = spatial_gating(u, z, g_sgu, w_sp, b_sp)
    out_lat = jnp.concatenate([att, sg], axis=-1) @ w_out
    if not need_ctx:
        return out_lat, None
    qc = hc @ w_in[:, :Q_DIM]
    uc, zc = jnp.split(hc @ w_in[:, Q_DIM + 2 * KV_DIM:], 2, axis=-1)
    att_c = context_attention(qc, kc, vc, sink)
    sg_c = spatial_gating(uc, zc, g_sgu, w_sp, b_sp)
    return out_lat, jnp.concatenate([att_c, sg_c], axis=-1) @ w_out

def short_conv_mixer(h, w_in, conv_w, w_out):
    bg, cg, xt = jnp.split(h @ w_in, 3, axis=-1)
    y = cg * xt
    yp = jnp.pad(y, ((0, 0), (1, 1), (0, 0)))
    conv = yp[:, :-2] * conv_w[0] + yp[:, 1:-1] * conv_w[1] + yp[:, 2:] * conv_w[2]
    return (bg * conv) @ w_out

def moe_ffn(h, w_rg, b_rg, w_re, b_re, w_gate, w_up, w_down):
    n, d = h.shape
    f32 = jnp.float32
    g_logits = jnp.einsum('nd,dg->ng', h, w_rg, preferred_element_type=f32) + b_rg.astype(f32)
    g_idx = jnp.argmax(g_logits, axis=-1).astype(jnp.int32)
    g_w = jnp.take_along_axis(jax.nn.softmax(g_logits, axis=-1), g_idx[:, None], axis=-1)
    e_logits = (jnp.einsum('nd,de->ne', h, w_re, preferred_element_type=f32) + b_re.astype(f32))
    e_logits = e_logits.reshape(n, N_GROUPS, EXPERTS_PER_GROUP)
    e_sel = jnp.take_along_axis(e_logits, g_idx[:, None, None], axis=1)[:, 0]
    top_v, top_i = lax.top_k(e_sel, TOP_K_IN_GROUP)
    gate = g_w * jax.nn.softmax(top_v, axis=-1)
    expert = g_idx[:, None] * EXPERTS_PER_GROUP + top_i.astype(jnp.int32)
    n_assign = n * TOP_K_IN_GROUP
    flat_e = expert.reshape(-1)
    flat_tok = jnp.repeat(jnp.arange(n, dtype=jnp.int32), TOP_K_IN_GROUP)
    flat_w = gate.reshape(-1).astype(h.dtype)
    order = jnp.argsort(flat_e)
    sorted_e = flat_e[order]
    counts = jnp.bincount(flat_e, length=N_EXPERTS)
    padded = (counts + MOE_BLOCK - 1) // MOE_BLOCK * MOE_BLOCK
    pad_end = jnp.cumsum(padded)
    pad_start = pad_end - padded
    raw_start = jnp.cumsum(counts) - counts
    dest = pad_start[sorted_e] + jnp.arange(n_assign, dtype=pad_start.dtype) - raw_start[sorted_e]
    n_blocks = -(-n_assign // MOE_BLOCK) + N_EXPERTS
    n_rows = n_blocks * MOE_BLOCK
    row_tok = jnp.zeros((n_rows,), jnp.int32).at[dest].set(flat_tok[order])
    row_w = jnp.zeros((n_rows,), h.dtype).at[dest].set(flat_w[order])
    block_e = jnp.clip(jnp.searchsorted(pad_end, jnp.arange(n_blocks, dtype=pad_end.dtype) * MOE_BLOCK, side='right'), 0, N_EXPERTS - 1)
    xb = h[row_tok].reshape(n_blocks, MOE_BLOCK, d)

    def expert_block(args):
        xblk, e = args
        hid = jax.nn.silu(xblk @ w_gate[e]) * (xblk @ w_up[e])
        return hid @ w_down[e]

    yb = lax.map(expert_block, (xb, block_e)).reshape(n_rows, d)
    return jnp.zeros_like(h).at[row_tok].add(yb * row_w[:, None])

def second_inputs(seed: int = 0) -> dict:
    key = jax.random.key(seed)
    ks = jax.random.split(key, 25)
    D = D_MODEL

    def nrm(k, shape, s):
        return jax.random.normal(k, shape, jnp.float32) * s

    return {
        'x': nrm(ks[0], (BATCH, SEQ, D), 1.0),
        'c': nrm(ks[1], (BATCH, D), 1.0),
        'ctx': nrm(ks[2], (BATCH, CTX_LEN, D), 1.0),
        'c_ctx': nrm(ks[3], (D,), 1.0),
        'w_ada': nrm(ks[4], (DEPTH, D, 6 * D), 0.5 * D ** -0.5),
        'b_ada': nrm(ks[5], (DEPTH, 6 * D), 0.02),
        'g_norm1': 1.0 + nrm(ks[6], (DEPTH, D), 0.1),
        'g_norm2': 1.0 + nrm(ks[7], (DEPTH, D), 0.1),
        'g_final': 1.0 + nrm(ks[8], (D,), 0.1),
        'w_in_even': nrm(ks[9], (N_EVEN_2, D, EVEN_IN), D ** -0.5),
        'attn_sink': nrm(ks[10], (N_EVEN_2, N_Q_HEADS), 1.0),
        'g_sgu': 1.0 + nrm(ks[11], (N_EVEN_2, SG_WIDTH), 0.1),
        'w_spatial': nrm(ks[12], (N_EVEN_2, SG_GROUPS, SG_CHUNK, SG_CHUNK), SG_CHUNK ** -0.5),
        'b_spatial': 1.0 + nrm(ks[13], (N_EVEN_2, SG_GROUPS, SG_CHUNK), 0.1),
        'w_out_even': nrm(ks[14], (N_EVEN_2, EVEN_MIX, D), EVEN_MIX ** -0.5),
        'w_in_odd': nrm(ks[15], (N_ODD_2, D, 3 * CONV_WIDTH), D ** -0.5),
        'conv_w': nrm(ks[16], (N_ODD_2, CONV_K, CONV_WIDTH), CONV_K ** -0.5),
        'w_out_odd': nrm(ks[17], (N_ODD_2, CONV_WIDTH, D), CONV_WIDTH ** -0.5),
        'w_router_group': nrm(ks[18], (DEPTH, D, N_GROUPS), D ** -0.5),
        'b_router_group': nrm(ks[19], (DEPTH, N_GROUPS), 0.01),
        'w_router_expert': nrm(ks[20], (DEPTH, D, N_EXPERTS), D ** -0.5),
        'b_router_expert': nrm(ks[21], (DEPTH, N_EXPERTS), 0.01),
        'w_gate': nrm(ks[22], (DEPTH, N_EXPERTS, D, EXPERT_HIDDEN), D ** -0.5),
        'w_up': nrm(ks[23], (DEPTH, N_EXPERTS, D, EXPERT_HIDDEN), D ** -0.5),
        'w_down': nrm(ks[24], (DEPTH, N_EXPERTS, EXPERT_HIDDEN, D), EXPERT_HIDDEN ** -0.5),
    }

def second_block(x, c, ctx, c_ctx, w_ada, b_ada, g_norm1, g_norm2, g_final, w_in_even, attn_sink, g_sgu,
              w_spatial, b_spatial, w_out_even, w_in_odd, conv_w, w_out_odd, w_router_group,
              b_router_group, w_router_expert, b_router_expert, w_gate, w_up, w_down):
    b, s, d = x.shape
    rows = s // GRID_W
    rope = axial_rope_tables(rows, x.dtype)
    silu_c = jax.nn.silu(c)
    silu_cc = jax.nn.silu(c_ctx)
    lat, cx = x, ctx
    for l in range(DEPTH):
        need_ctx = any(j % 2 == 0 for j in range(l + 1, DEPTH))
        m = jnp.split(silu_c @ w_ada[l] + b_ada[l], 6, axis=-1)
        sh1, sc1, g1, sh2, sc2, g2 = [t[:, None, :] for t in m]
        h = modulate(rms_norm(lat, g_norm1[l]), sh1, sc1)
        mix_c = None
        if l % 2 == 0 or need_ctx:
            csh1, csc1, cg1, csh2, csc2, cg2 = jnp.split(silu_cc @ w_ada[l] + b_ada[l], 6, axis=-1)
            hc = modulate(rms_norm(cx, g_norm1[l]), csh1, csc1)
        i = l // 2
        if l % 2 == 0:
            mix, mix_c = even_mixer(h, hc, w_in_even[i], attn_sink[i], g_sgu[i], w_spatial[i],
                                    b_spatial[i], w_out_even[i], rope, need_ctx)
        else:
            mix = short_conv_mixer(h, w_in_odd[i], conv_w[i], w_out_odd[i])
            if need_ctx:
                mix_c = short_conv_mixer(hc, w_in_odd[i], conv_w[i], w_out_odd[i])
        lat = lat + g1 * mix
        h2 = modulate(rms_norm(lat, g_norm2[l]), sh2, sc2)
        lat = lat + g2 * moe_ffn(h2.reshape(-1, d), w_router_group[l], b_router_group[l], w_router_expert[l],
                                 b_router_expert[l], w_gate[l], w_up[l], w_down[l]).reshape(b, s, d)
        if need_ctx:
            cx = cx + cg1 * mix_c
            hc2 = modulate(rms_norm(cx, g_norm2[l]), csh2, csc2)
            cx = cx + cg2 * moe_ffn(hc2.reshape(-1, d), w_router_group[l], b_router_group[l], w_router_expert[l],
                                    b_router_expert[l], w_gate[l], w_up[l], w_down[l]).reshape(cx.shape)
    return rms_norm(lat, g_final)


def setup_inputs(seed=0):
    out = dict(first_inputs(seed))
    for name, value in second_inputs(seed + 1).items():
        if name != "x":
            out[name + "_2"] = value
    return out


def reference(
    x, pre_mix_g, post_mix_g, pre_ffn_g, post_ffn_g, ab_w_in, ab_b_in, conf_conv_w, conf_conv_b,
    conf_ln_g, conf_ln_b, lru_conv_w, lru_conv_b, lru_w_a, lru_b_a, lru_w_x, lru_b_x,
    lru_lambda, ab_w_out, ml_w_in, ml_b_in, ml_head_g, ml_w_out, ffn_w_gate, ffn_w_up,
    ffn_w_down, c_2, ctx_2, c_ctx_2, w_ada_2, b_ada_2, g_norm1_2, g_norm2_2, g_final_2,
    w_in_even_2, attn_sink_2, g_sgu_2, w_spatial_2, b_spatial_2, w_out_even_2, w_in_odd_2,
    conv_w_2, w_out_odd_2, w_router_group_2, b_router_group_2, w_router_expert_2,
    b_router_expert_2, w_gate_2, w_up_2, w_down_2,
):
    x = first_block(
        x, pre_mix_g, post_mix_g, pre_ffn_g, post_ffn_g, ab_w_in, ab_b_in, conf_conv_w,
        conf_conv_b, conf_ln_g, conf_ln_b, lru_conv_w, lru_conv_b, lru_w_a, lru_b_a, lru_w_x,
        lru_b_x, lru_lambda, ab_w_out, ml_w_in, ml_b_in, ml_head_g, ml_w_out, ffn_w_gate,
        ffn_w_up, ffn_w_down,
    )
    return second_block(
        x, c_2, ctx_2, c_ctx_2, w_ada_2, b_ada_2, g_norm1_2, g_norm2_2, g_final_2, w_in_even_2,
        attn_sink_2, g_sgu_2, w_spatial_2, b_spatial_2, w_out_even_2, w_in_odd_2, conv_w_2,
        w_out_odd_2, w_router_group_2, b_router_group_2, w_router_expert_2, b_router_expert_2,
        w_gate_2, w_up_2, w_down_2,
    )


_drawn_inputs = setup_inputs


def setup_inputs(seed=0):
    import zlib

    import numpy as np

    out = dict(_drawn_inputs(seed))
    spreads = {}
    factors = {'lru_b_a': 8.0,
     'lru_b_x': 8.0,
     'ctx_2': 6.314,
     'c_ctx_2': 2.826,
     'b_ada_2': 2.928,
     'g_norm2_2': 3.016,
     'attn_sink_2': 8.0,
     'g_sgu_2': 6.092,
     'b_spatial_2': 6.629,
     'b_router_group_2': 8.0,
     'b_router_expert_2': 8.0}
    for name, (base, spread) in spreads.items():
        noise = np.random.default_rng([zlib.crc32(name.encode()), seed]).standard_normal(out[name].shape)
        drawn = base * np.exp(spread * noise) if base else spread * noise
        out[name] = __import__('jax').numpy.asarray(drawn.astype(out[name].dtype))
    for name, factor in factors.items():
        out[name] = (out[name] * factor).astype(out[name].dtype)
    return out
```

```python
from contextlib import ExitStack

import concourse.bass as bass
from concourse import mybir

F32 = mybir.dt.float32
ALU = mybir.AluOpType
ACT = mybir.ActivationFunctionType
AX = mybir.AxisListType.X

P = 128
D = 1024
KT = D // P
T = 256
TT = T // P
DFF = 2816
FT = DFF // P
CH = 512
RING = 6
SLOT = KT * CH
EPS = 1e-6
WORK = 12080
HALF = 512
HTL = HALF // P
CK = 31
LK = 4
HEADS = 8
NEXP = 32
NGRP = 4
EPG = NEXP // NGRP
NLOG = NGRP + NEXP
EH = 512
BIG = 1e30
LRU_C = 8.0

VEC_SIZES = [("pre_mix_g", 16), ("post_mix_g", 16), ("pre_ffn_g", 16), ("post_ffn_g", 16), ("ab_b_in", 16),
             ("conf_w", 4 * CK), ("conf_b", 4), ("ln_g", 4), ("ln_b", 4), ("lru_w", 4 * LK), ("lru_b", 4),
             ("b_a", 4), ("b_x", 4), ("lam", 4), ("ml_b", 16), ("head_g", 8), ("c", 16), ("b_ada", 96),
             ("g_norm1", 16), ("g_norm2", 16), ("g_final", 8), ("conv_w", 8 * 3)]
VEC = {}
_at = 0
for _n, _s in VEC_SIZES:
    VEC[_n] = (_at, _s)
    _at += _s
NVEC = _at
CONST_SIZES = [("ident", P), ("cos", T), ("sin", T), ("perm", 5 * P), ("tri", T), ("window", TT * 2 * T)]
CON = {}
_at = 0
for _n, _s in CONST_SIZES:
    CON[_n] = (_at, _s)
    _at += _s
NCON = _at
ROW_SIZES = [("v_b", D), ("gate_b", 16), ("router_b", 2 * NLOG), ("g_sgu", HALF), ("sink", 8)]
ROW = {}
_at = 0
for _n, _s in ROW_SIZES:
    ROW[_n] = (_at, _s)
    _at += _s
NROW = _at
SELS = (8 + 4) * P


class Turns:

    def __init__(self, engine):
        self.engine, self.given, self.taken = engine, {}, {}

    def give(self, instruction, sem):
        instruction.then_inc(sem, 1)
        self.given[sem] = self.given.get(sem, 0) + 1

    def take(self, sem, n=1):
        self.taken[sem] = self.taken.get(sem, 0) + n
        self.engine.wait_ge(sem, self.taken[sem])

    def own(self, sem, but=0):
        if self.given[sem] > but:
            self.engine.wait_ge(sem, self.given[sem] - but)


def build(nc, a, out):
    with ExitStack() as ctx:
        def sb(name, shape):
            return ctx.enter_context(nc.sbuf_tensor(name, shape, F32))

        def sem(name):
            return ctx.enter_context(nc.semaphore(name))

        ring = sb("ring", [P, RING, SLOT])
        x = sb("x", [P, KT, T])
        h = sb("h", [P, KT, T])
        sq = sb("sq", [P, KT, T])
        work = sb("work", [P, WORK])
        vec = sb("vec", [P, NVEC])
        con = sb("con", [P, NCON])
        misc = sb("misc", [33, NROW])
        ones = sb("ones", [P, P])
        zeros = sb("zeros", [P, T])
        bd = sb("bd", [P, 2, HTL, P])
        gw = sb("gw", [P, KT, 16])
        rw = sb("rw", [P, 2, KT, NLOG])
        wsp = sb("wsp", [P, HEADS, P])
        bsp = sb("bsp", [HEADS, P])
        sgu_g = sb("sgu_g", [P, HALF])
        sink = sb("sink", [P, 8])
        silu_c = sb("silu_c", [P, KT, 2])
        ada = sb("ada", [P, 2, 48, 2])
        scale_g = sb("scale_g", [P, 5, KT])
        rstd = sb("rstd", [P, T])
        root = sb("root", [P, T])
        root_c = sb("root_c", [P, T])
        eps = sb("eps", [P, 1])
        small = sb("small", [P, 64])
        lamt = sb("lamt", [P, 32])
        tmp = sb("tmp", [P, 2, T])
        ps = ctx.enter_context(nc.psum_tensor("ps", [P, 8, 512], F32))

        def v(name):
            return vec[:, VEC[name][0]:VEC[name][0] + VEC[name][1]]

        def cst(name, n=P):
            return con[0:n, CON[name][0]:CON[name][0] + CON[name][1]]

        def rowv(name):
            return misc[32:33, ROW[name][0]:ROW[name][0] + ROW[name][1]]

        def region(at, *shape, n=P):
            size = 1
            for s in shape:
                size *= s
            assert at + size <= WORK
            w = work[0:n, at:at + size]
            if len(shape) == 2:
                return w.rearrange("p (a b) -> p a b", a=shape[0])
            return w

        ident = cst("ident")
        cos, sin = cst("cos"), cst("sin")
        perm = cst("perm").rearrange("p (a b) -> p a b", a=5)
        tri = cst("tri")
        window = cst("window").rearrange("p (a b) -> p a b", a=TT)
        sel8 = misc[0:8, 0:8 * P].rearrange("p (a b) -> p a b", a=8)
        selb = misc[0:8, 8 * P:SELS].rearrange("p (a b) -> p a b", a=4)
        ones_row = ones[32:33, :]

        sgate = region(0, HTL, T)
        cpad = region(1024, HTL, CK - 1 + T)
        rpad = region(2168, HTL, LK - 1 + T)
        gin = region(3204, HTL, T)
        xr = region(4228, HTL, T)
        th = region(5252, HTL, T)
        den_a = region(6276, HTL, T)
        bx = region(7300, HTL, T)
        cv = region(8324, HTL, T)
        ymix = region(9348, KT, T)
        ff = region(0, FT, T)
        sgt = region(FT * T, 2, T)
        fft = region(FT * T + 2 * T, 2, T)
        q_m = region(0, HTL, T)
        k_m = region(1024, HTL, T)
        v_m = region(2048, TT, D)
        so = region(4096, KT, T)
        y_m = region(6144, KT, T)
        darg = region(8192, 2, 384)
        dexp = region(8960, 2, 384)
        pm = region(9728, 2, 384)
        absd = region(10496, 2, T)
        gtok = region(11008, TT, 16)
        acol = region(11040, TT, 8)
        ghead = region(11056, 4, T, n=8)
        ctxr = region(0, KT, T)
        hc = region(2048, KT, T)
        q_a = region(0, HTL, T)
        u_a = region(1024, HTL, T)
        z_a = region(2048, TT, HALF)
        zc = region(3072, TT, HALF)
        kd = region(4096, 2, 2 * T)
        v_a = region(5120, 4, P)
        kraw = region(5632, 2, T)
        rope_t = region(6144, 2, T)
        mix = region(6656, KT, T)
        sm = region(8704, 2, 2 * T)
        pt = region(9728, 2, 2 * T)
        pexp = region(10752, 2, 2 * T)
        bg = region(0, KT, T)
        cg = region(2048, KT, T)
        ypad = region(4096, KT, T + 2)
        cvo = region(6160, KT, T)
        lg = region(0, TT, NLOG)
        G = region(72, TT, NEXP)
        rt = region(136, 6, NEXP)
        hid = region(512, 2, HTL * T)
        esg = region(2560, 2, T)
        et = region(3072, 2, T)
        dg = region(3584, 2, T)
        gb = region(4096, 2, T)

        consts_loaded = sem("consts_loaded")
        x_loaded = sem("x_loaded")
        ctx_loaded = sem("ctx_loaded")
        blocks_loaded = sem("blocks_loaded")
        slot_loaded = [sem(f"slot{s}_loaded") for s in range(RING)]
        tiles_act = sem("tiles_for_act")
        tiles_dve = sem("tiles_for_dve")
        memsets = sem("memsets_done")
        vchain = sem("vector_step_done")
        achain = sem("scalar_step_done")
        down_part = sem("down_part_done")
        out_stored = sem("out_stored")
        names = ("rows_spread c_sigmoid silu_c ada_raw squares roots x_ready x_added h_ready hc_ready glu_gate glu "
                 "rec_in gelu_in lru_conv lru_gate lam_abs lam_ln lam_rate lru_tanh lru_root conf_conv ln_mean "
                 "ln_centred ln_normed ln_sigmoid mixed proj_copied ffn_sig ffn_gate_read hidden kb_scaled mq mk mo mv "
                 "gates_tok gates_head f_abs f_ln gate_a gate_m gate_expm acol_ready exponents decays weighted absden "
                 "den_read head_out head_roots kraw_ready vals qraw_ready u_gelu z_gelu z_centred z_sq z_root z_normed "
                 "k_ctx k_rope_read q_rope_read rotated scores_read maxima exps probs pt_ready att_out logits_read "
                 "router_max router_exp router_done router_gap router_gexp cgate cvalue bgate").split()
        S = {n: sem(n) for n in names}
        layer_names = ("diag row_full row_copied gate_full gate_sig gate_freed up_full up_freed hid_ready "
                       "down_done").split()
        E = [{n: sem(f"expert_{n}_{l}") for n in layer_names} for l in range(2)]

        chunks = []

        def chunk(src, nk=KT, cols=CH):
            chunks.append((src, nk, cols))

        for c in (1, 0, 3, 2):
            chunk(a["ab_w_in"][c])
        for c in range(12):
            chunk(a["w_ada"][0, c])
        for c in range(2):
            chunk(a["ab_w_out"][c])

        def ffn_chunks(l):
            for c in range(6):
                n = min(CH, DFF - c * CH)
                chunk(a["w_ff_gate"][l, c, :, :, 0:n], cols=n)
                chunk(a["w_ff_up"][l, c, :, :, 0:n], cols=n)
            for c in range(2):
                for k0 in range(0, FT, KT):
                    nk = min(KT, FT - k0)
                    chunk(a["w_ff_down"][l, c, :, k0:k0 + nk, :], nk=nk)

        ffn_chunks(0)
        for c in (0, 1, 4, 5, 2, 3):
            chunk(a["ml_w_in"][c])
        for c in range(12):
            chunk(a["w_ada"][1, c])
        for c in range(2):
            chunk(a["ml_w_out"][c])
        ffn_chunks(1)
        chunk(a["w_even_kv"], cols=256)
        for c in range(3):
            chunk(a["w_even"][c])
        for c in range(2):
            chunk(a["w_even_out"][c])
        moe_first = [len(chunks)]
        for n in range(3 * NEXP):
            chunk(None)
        for c in (2, 4, 3, 5, 0, 1):
            chunk(a["w_odd"][c])
        for c in range(2):
            chunk(a["w_odd_out"][c])
        moe_first.append(len(chunks))
        for n in range(3 * NEXP):
            chunk(None)
        released = {}
        bank_of = {tiles_act: [], tiles_dve: []}
        h_count = []
        gate_bank = []

        block = ctx.enter_context(nc.Block())

        @block.tensor
        def _(pe):
            turn = Turns(pe)
            freed = {}
            owner = [None] * 8
            state = {"chunk": 0, "bank": 0, "stat": 0}
            mm = nc.tensor.matmul

            def open_bank(b):
                if owner[b] is not None:
                    pe.wait_ge(*owner[b])

            def close_bank(b, last, full, free, reads=1):
                turn.give(last, full)
                bank_of[full].append(b)
                freed[free] = freed.get(free, 0) + reads
                owner[b] = (free, freed[free])

            def next_bank():
                state["bank"] = (state["bank"] + 1) % 4
                open_bank(state["bank"])
                return state["bank"]

            def stat_bank():
                state["stat"] ^= 1
                open_bank(4 + state["stat"])
                return 4 + state["stat"]

            def next_chunk():
                n = state["chunk"]
                state["chunk"] += 1
                pe.wait_ge(slot_loaded[n % RING], 16 * (n // RING + 1))
                _, nk, cols = chunks[n]
                return n, ring[:, n % RING, 0:nk * cols].rearrange("p (k c) -> p k c", k=nk)

            def release(n, full):
                released[n] = (full, turn.given[full])

            def product(w, m, rhs, full, free, ready=None, nready=KT):
                b = next_bank()
                nk = rhs.shape[1]
                for k in range(nk):
                    if ready is not None and k < nready:
                        turn.take(ready)
                    last = mm(ps[:, b, 0:T], w[:, k, m * P:(m + 1) * P], rhs[:, k, :],
                              start=(k == 0), stop=(k == nk - 1))
                close_bank(b, last, full, free)
                return b

            def dense(rhs, full, free, ready=None, nready=KT):
                n, w = next_chunk()
                for m in range(w.shape[2] // P):
                    product(w, m, rhs, full, free, ready, nready)
                    ready = None
                release(n, full)

            def stats(n=KT):
                b = stat_bank()
                for k in range(n):
                    turn.take(S["squares"])
                    last = mm(ps[:, b, 0:T], ones[:], sq[:, k, :], start=(k == 0), stop=(k == n - 1))
                close_bank(b, last, tiles_act, S["roots"])

            def ada_chunk():
                n, w = next_chunk()
                b = stat_bank()
                for m in range(4):
                    for k in range(KT):
                        last = mm(ps[:, b, 2 * m:2 * m + 2], w[:, k, m * P:(m + 1) * P], silu_c[:, k, :],
                                  start=(k == 0), stop=(k == KT - 1))
                close_bank(b, last, tiles_act, S["ada_raw"])
                release(n, tiles_act)

            pe.wait_ge(consts_loaded, 16 * 8)
            pe.wait_ge(memsets, 6)
            b = stat_bank()
            close_bank(b, mm(ps[:, b, 0:HALF], ones_row, rowv("g_sgu"), start=True, stop=True),
                       tiles_act, S["rows_spread"])
            b = stat_bank()
            close_bank(b, mm(ps[:, b, 0:8], ones_row, rowv("sink"), start=True, stop=True),
                       tiles_act, S["rows_spread"])

            stats()
            dense(h, tiles_act, S["glu_gate"], S["h_ready"])
            dense(h, tiles_dve, S["glu"])
            dense(h, tiles_act, S["rec_in"])
            dense(h, tiles_act, S["gelu_in"])
            turn.take(S["silu_c"])
            for c in range(2):
                ada_chunk()
            pe.wait_ge(blocks_loaded, 64)
            for j in range(HTL):
                turn.take(S["lru_conv"])
                for g in range(2):
                    b = next_bank()
                    close_bank(b, mm(ps[:, b, 0:T], bd[:, g, j, :], xr[:, j, :], start=True, stop=True),
                               tiles_act, S["lru_gate"])
            for c in range(10):
                ada_chunk()
            b = stat_bank()
            for j in range(HTL):
                turn.take(S["conf_conv"])
                last = mm(ps[:, b, 0:T], ones[:], cv[:, j, :], start=(j == 0), stop=(j == HTL - 1))
            close_bank(b, last, tiles_dve, S["ln_mean"])
            stats(HTL)

            def project_norm(src, nready):
                dense(src, tiles_act, S["proj_copied"], S["mixed"], nready)
                dense(src, tiles_act, S["proj_copied"])
                stats()

            project_norm(ymix, HTL)

            def ffn():
                stats()
                ready = S["h_ready"]
                for c in range(6):
                    ng, wg = next_chunk()
                    nu, wu = next_chunk()
                    for m in range(wg.shape[2] // P):
                        gate_bank.append(product(wg, m, h, tiles_act, S["ffn_gate_read"], ready))
                        ready = None
                        product(wu, m, h, tiles_dve, S["hidden"])
                    release(ng, tiles_dve)
                    release(nu, tiles_dve)
                for c in range(2):
                    for b in range(4):
                        open_bank(b)
                    for k0 in range(0, FT, KT):
                        n, w = next_chunk()
                        nk = w.shape[1]
                        for m in range(4):
                            for k in range(k0, k0 + nk):
                                if c == 0 and m == 0:
                                    turn.take(S["hidden"])
                                last = mm(ps[:, m, 0:T], w[:, k - k0, m * P:(m + 1) * P], ff[:, k, :],
                                          start=(k == 0), stop=(k == FT - 1))
                            if k0 + nk == FT:
                                close_bank(m, last, tiles_act, S["proj_copied"])
                        if k0 + nk < FT:
                            turn.give(last, down_part)
                        release(n, down_part if k0 + nk < FT else tiles_act)
                state["bank"] = 3
                stats()

            ffn()

            stats()
            dense(h, tiles_act, S["mq"], S["h_ready"])
            dense(h, tiles_act, S["mk"])
            b = stat_bank()
            for t in range(TT):
                for k in range(KT):
                    mm(ps[:, b, 16 * t:16 * t + 16], h[:, k, t * P:(t + 1) * P], gw[:, k, :],
                       start=(k == 0), stop=False)
                last = mm(ps[:, b, 16 * t:16 * t + 16], ones_row, rowv("gate_b"), start=False, stop=True)
            close_bank(b, last, tiles_dve, S["gates_tok"])
            for c in range(2):
                dense(h, tiles_act, S["mo"])
            turn.take(S["gates_tok"])
            b = stat_bank()
            for g in range(2):
                for t in range(TT):
                    last = nc.tensor.transpose(ps[0:8, b, (2 * g + t) * P:(2 * g + t + 1) * P],
                                               gtok[:, t, 8 * g:8 * g + 8], ident)
            close_bank(b, last, tiles_dve, S["gates_head"])
            for c in range(2):
                n, w = next_chunk()
                for t in range(TT):
                    b = next_bank()
                    for k in range(KT):
                        mm(ps[:, b, :], h[:, k, t * P:(t + 1) * P], w[:, k, :], start=(k == 0), stop=False)
                    last = mm(ps[:, b, :], ones_row, rowv("v_b")[:, c * CH:(c + 1) * CH], start=False, stop=True)
                    close_bank(b, last, tiles_act, S["mv"])
                release(n, tiles_act)
            for c in range(4):
                ada_chunk()
            turn.take(S["gate_a"])
            b = stat_bank()
            for t in range(TT):
                last = nc.tensor.transpose(ps[:, b, 8 * t:8 * t + 8], ghead[:, 0, t * P:(t + 1) * P],
                                           ident[0:8, 0:8])
            close_bank(b, last, tiles_dve, S["acol_ready"])

            def head_scores(n):
                b = next_bank()
                close_bank(b, mm(ps[:, b, 0:T], sel8[:, n, :], ghead[:, 2, :], start=True, stop=True),
                           tiles_dve, S["exponents"])
                b = next_bank()
                lo = 64 * (n % 2)
                kk, qq = k_m[lo:lo + 64, n // 2, :], q_m[lo:lo + 64, n // 2, :]
                mm(ps[:, b, 0:T], kk[:, 0:P], qq, start=True, stop=True)
                close_bank(b, mm(ps[:, b, T:T + P], kk[:, P:T], qq[:, P:T], start=True, stop=True),
                           tiles_dve, S["weighted"])

            turn.take(S["gate_expm"])
            turn.take(S["mq"], 4)
            turn.take(S["mk"], 4)
            turn.take(S["mv"], 4)
            head_scores(0)
            for n in range(HEADS):
                if n + 1 < HEADS:
                    head_scores(n + 1)
                ada_chunk()
                turn.take(S["weighted"])
                open_bank(7)
                mm(ps[:, 7, T:2 * T], sel8[:, n, :], ghead[:, 3, :], start=True, stop=True)
                mm(ps[:, 7, 0:T], ones[:], pm[:, n % 2, 0:T], start=True, stop=False, skip_group_check=True)
                close_bank(7, mm(ps[:, 7, P:T], ones[:], pm[:, n % 2, T:T + P], start=False, stop=True,
                                 skip_group_check=True), tiles_act, S["den_read"])
                open_bank(6)
                mm(ps[:, 6, 0:T], v_m[:, 0, n * P:(n + 1) * P], pm[:, n % 2, 0:T], start=True, stop=False,
                   skip_group_check=True)
                close_bank(6, mm(ps[:, 6, P:T], v_m[:, 1, n * P:(n + 1) * P], pm[:, n % 2, T:T + P],
                                 start=False, stop=True, skip_group_check=True), tiles_dve, S["head_out"])
            for n in range(HEADS):
                turn.take(S["squares"])
                b = stat_bank()
                close_bank(b, mm(ps[:, b, 0:T], ones[:], sq[:, n, :], start=True, stop=True),
                           tiles_act, S["head_roots"])
            project_norm(y_m, KT)
            ffn()

            stats()
            stats()
            n, w = next_chunk()
            product(w, 0, hc, tiles_act, S["kraw_ready"], S["hc_ready"])
            product(w, 0, h, tiles_act, S["kraw_ready"], S["h_ready"])
            b = next_bank()
            for t in range(4):
                src = hc if t < 2 else h
                for k in range(KT):
                    last = mm(ps[:, b, t * P:(t + 1) * P], src[:, k, (t % 2) * P:(t % 2 + 1) * P],
                              w[:, k, P:2 * P], start=(k == 0), stop=(k == KT - 1))
            close_bank(b, last, tiles_act, S["vals"])
            release(n, tiles_act)
            dense(h, tiles_act, S["qraw_ready"])
            dense(h, tiles_act, S["u_gelu"])
            n, w = next_chunk()
            for t in range(TT):
                b = next_bank()
                for k in range(KT):
                    last = mm(ps[:, b, :], h[:, k, t * P:(t + 1) * P], w[:, k, :], start=(k == 0), stop=(k == KT - 1))
                close_bank(b, last, tiles_act, S["z_gelu"])
            release(n, tiles_act)
            turn.take(S["kraw_ready"], 2)
            for kv in range(2):
                b = next_bank()
                close_bank(b, mm(ps[:, b, 0:T], perm[:, 1 + kv, :], kraw[:, 0, :], start=True, stop=True),
                           tiles_act, S["k_ctx"])
                b = next_bank()
                mm(ps[:, b, 0:T], perm[:, 1 + kv, :], kraw[:, 1, :], start=True, stop=True)
                close_bank(b, mm(ps[:, b, T:2 * T], perm[:, 3 + kv, :], kraw[:, 1, :], start=True, stop=True),
                           tiles_dve, S["k_rope_read"])
            turn.take(S["qraw_ready"], 4)
            for j in range(HTL):
                b = next_bank()
                close_bank(b, mm(ps[:, b, 0:T], perm[:, 0, :], q_a[:, j, :], start=True, stop=True),
                           tiles_dve, S["q_rope_read"])

            def att_scores(i):
                n, t = i // 2, i % 2
                lo = 64 * (n % 2)
                b = next_bank()
                close_bank(b, mm(ps[:, b, :], q_a[lo:lo + 64, n // 2, t * P:(t + 1) * P], kd[lo:lo + 64, n // 4, :],
                                 start=True, stop=True), tiles_dve, S["scores_read"])

            turn.take(S["k_ctx"], 2)
            turn.take(S["vals"])
            turn.take(S["rotated"])
            att_scores(0)
            for i in range(2 * HEADS):
                if i + 1 < 2 * HEADS:
                    att_scores(i + 1)
                n, t = i // 2, i % 2
                turn.take(S["probs"])
                b = stat_bank()
                for k in range(4):
                    last = nc.tensor.transpose(ps[:, b, k * P:(k + 1) * P], pexp[:, i % 2, k * P:(k + 1) * P], ident)
                close_bank(b, last, tiles_act, S["pt_ready"])
                turn.take(S["pt_ready"])
                b = 6 + (n // 2) % 2
                if i % 4 == 0:
                    open_bank(b)
                lo = 64 * (n % 2)
                for k in range(4):
                    last = mm(ps[lo:lo + 64, b, t * P:(t + 1) * P], v_a[:, k, 64 * (n // 4):64 * (n // 4) + 64],
                              pt[:, i % 2, k * P:(k + 1) * P], start=(k == 0), stop=(k == 3))
                if i % 4 == 3:
                    close_bank(b, last, tiles_act, S["att_out"])
            turn.take(S["z_normed"])
            for j in range(HTL):
                b = next_bank()
                for t in range(TT):
                    mm(ps[:, b, t * P:(t + 1) * P], selb[:, j, :], bsp[:], start=True, stop=False,
                       skip_group_check=True)
                    for i in range(2):
                        last = mm(ps[64 * i:64 * i + 64, b, t * P:(t + 1) * P],
                                  z_a[:, t, (2 * j + i) * 64:(2 * j + i + 1) * 64], wsp[:, 2 * j + i, :],
                                  start=False, stop=True, skip_group_check=True)
                close_bank(b, last, tiles_dve, S["mixed"])

            def latent_project(src):
                dense(src, tiles_dve, S["x_added"])
                dense(src, tiles_dve, S["x_added"])
                stats()

            turn.take(S["att_out"], 4)
            turn.take(S["mixed"], 4)
            latent_project(mix)

            def experts(l):
                e_ = E[l]
                b = stat_bank()
                for t in range(TT):
                    for k in range(KT):
                        if t == 0:
                            turn.take(S["h_ready"])
                        mm(ps[:, b, NLOG * t:NLOG * (t + 1)], h[:, k, t * P:(t + 1) * P], rw[:, l, k, :],
                           start=(k == 0), stop=False)
                    last = mm(ps[:, b, NLOG * t:NLOG * (t + 1)], ones_row,
                              rowv("router_b")[:, NLOG * l:NLOG * (l + 1)], start=False, stop=True)
                close_bank(b, last, tiles_dve, S["logits_read"])
                for b in range(8):
                    open_bank(b)
                for b in range(4, 8):
                    mm(ps[:, b, :], zeros[:, 0:P], con[:, 0:512], start=True, stop=False, skip_group_check=True)
                first = moe_first[l]
                assert first == state["chunk"]
                with pe.Fori(0, NEXP // 2) as i:
                    for e in range(2):
                        slots = [(first + 3 * e + j) % RING for j in range(3)]
                        loads = [16 * ((first + 3 * e + j) // RING + 1) for j in range(3)]
                        pe.wait_ge(e_["diag"], 2 * i + e + 1)
                        pe.wait_ge(e_["row_copied"], 2 * i + e + 1)
                        mm(ps[:, 3, 0:P], ones[:], dg[:, e, 0:P], start=True, stop=True)
                        mm(ps[:, 3, P:T], ones[:], dg[:, e, P:T], start=True, stop=True).then_inc(e_["row_full"], 1)
                        pe.wait_ge(slot_loaded[slots[0]], 16 * i + loads[0])
                        pe.wait_ge(slot_loaded[slots[1]], 16 * i + loads[1])
                        wg, wu, wd = (ring[:, slots[j], :].rearrange("p (k c) -> p k c", k=KT if j < 2 else HTL)
                                      for j in range(3))
                        for m in range(HTL):
                            pe.wait_ge(e_["gate_freed"], 8 * i + 4 * e + m + 1)
                            for k in range(KT):
                                last = mm(ps[:, 2 * (m % 2), 0:T], wg[:, k, m * P:(m + 1) * P], h[:, k, :],
                                          start=(k == 0), stop=(k == KT - 1))
                            last.then_inc(e_["gate_full"], 1)
                            pe.wait_ge(e_["up_freed"], 8 * i + 4 * e + m + 1)
                            for k in range(KT):
                                last = mm(ps[:, 1, 0:T], wu[:, k, m * P:(m + 1) * P], h[:, k, :],
                                          start=(k == 0), stop=(k == KT - 1))
                            last.then_inc(e_["up_full"], 1)
                        pe.wait_ge(slot_loaded[slots[2]], 16 * i + loads[2])
                        for k in range(HTL):
                            pe.wait_ge(e_["hid_ready"], 8 * i + 4 * e + k + 1)
                            for m in range(KT):
                                last = mm(ps[:, 4 + m // 2, (m % 2) * T:(m % 2 + 1) * T],
                                          wd[:, k, m * P:(m + 1) * P], hid[:, e, k * T:(k + 1) * T],
                                          start=False, stop=False, skip_group_check=True)
                        last.then_inc(e_["down_done"], 1)
                state["chunk"] += 3 * NEXP
                for b in range(3):
                    owner[b] = (e_["hid_ready"], 4 * NEXP)
                owner[3] = (e_["row_copied"], NEXP + 1)
                for b in range(4, 8):
                    close_bank(b, mm(ps[:, b, :], zeros[:, 0:P], con[:, 0:512], start=False, stop=True,
                                     skip_group_check=True), tiles_dve, S["x_added"], reads=2)
                stats()

            experts(0)

            ready = S["h_ready"]
            for free, full in (("cgate", tiles_act), ("cvalue", tiles_dve)) * 2 + (("bgate", tiles_act),) * 2:
                dense(h, full, S[free], ready)
                ready = None
            for k in range(KT):
                turn.take(S["mixed"])
            latent_project(cvo)
            experts(1)

        @block.sync
        def _(sp):
            for dst, src in ((vec[:], a["vec"]), (con[:], a["con"]), (misc[32:33, :], a["row"]), (misc[0:8, 0:SELS], a["sel"]), (gw[:], a["gate_w"]),
                             (rw[:], a["router_w"]), (wsp[:], a["w_sp"]), (bsp[:], a["b_sp"])):
                sp.dma_start(dst, src).then_inc(consts_loaded, 16)

            def load(n):
                src, nk, cols = chunks[n]
                if n >= RING:
                    sp.wait_ge(*released[n - RING])
                sp.dma_start(ring[:, n % RING, 0:nk * cols].rearrange("p (k c) -> p k c", k=nk), src).then_inc(
                    slot_loaded[n % RING], 16)

            def load_experts(l):
                first, e_ = moe_first[l], E[l]
                weights = [a["w_gate"], a["w_up"], a["w_down"]]
                for j in range(6):
                    n = first + j
                    sp.wait_ge(*released[n - RING])
                    sp.dma_start(ring[:, n % RING, :], weights[j % 3][l, j // 3]).then_inc(slot_loaded[n % RING], 16)
                with sp.Fori(0, NEXP // 2 - 1) as i:
                    for e in range(2):
                        for j in range(3):
                            if j < 2:
                                sp.wait_ge(e_[("gate_full", "up_full")[j]], 8 * i + 4 * e + 4)
                            else:
                                sp.wait_ge(e_["down_done"], 2 * i + e + 1)
                            slot = (first + 3 * e + j) % RING
                            sp.dma_start(ring[:, slot, :], weights[j][l, 2 * i + (2 + e)]).then_inc(
                                slot_loaded[slot], 16)
                for e in range(NEXP - 2, NEXP):
                    released[first + 3 * e] = (e_["gate_full"], 4 * e + 4)
                    released[first + 3 * e + 1] = (e_["up_full"], 4 * e + 4)
                    released[first + 3 * e + 2] = (e_["down_done"], e + 1)

            for n in range(moe_first[0]):
                load(n)
            load_experts(0)
            for n in range(moe_first[0] + 3 * NEXP, moe_first[1]):
                load(n)
            load_experts(1)

        @block.gpsimd
        def _(pool):
            for dst, value in ((ones[:], 1.0), (bd[:], 0.0), (cpad[:, :, 0:CK - 1], 0.0), (rpad[:, :, 0:LK - 1], 0.0),
                               (eps[:], EPS), (zeros[:], 0.0)):
                nc.gpsimd.memset(dst, value).then_inc(memsets, 1)

        @block.scalar
        def _(act):
            turn = Turns(act)
            where = iter(bank_of[tiles_act])

            def A(out_, in_, f, bias=0.0, scale=1.0, **kw):
                return nc.scalar.activation(out_, in_, f, bias=bias, scale=scale, **kw)

            def tile():
                turn.take(tiles_act)
                return ps[:, next(where), :]

            def squares(src, ready=None, n=KT):
                for k in range(n):
                    if ready is not None:
                        turn.take(ready)
                    turn.give(A(sq[:, k, :], src[:, k, :], ACT.Square), S["squares"])

            def norm_root(count, to=root):
                turn.give(A(to[:], tile()[:, 0:T], ACT.Sqrt, bias=eps[:], scale=1.0 / count), S["roots"])

            def ada_out(l, c):
                turn.give(A(ada[:, l, 4 * c:4 * c + 4, :], tile()[:, 0:8].rearrange("p (a b) -> p a b", a=4),
                            ACT.Copy), S["ada_raw"])

            act.dma_start(x[:], a["x"]).then_inc(x_loaded, 16)
            act.wait_ge(memsets, 6)
            for g in range(2):
                for half in range(2):
                    act.dma_start(bd[64 * half:64 * half + 64, g, :, 64 * half:64 * half + 64],
                                  a["lru_w"][g, half]).then_inc(blocks_loaded, 16)
            act.wait_ge(consts_loaded, 16 * 8)
            turn.give(A(silu_c[:], v("c").rearrange("p (a b) -> p a b", b=2), ACT.Sigmoid), S["c_sigmoid"])
            turn.give(A(sgu_g[:], tile()[:, 0:HALF], ACT.Copy), S["rows_spread"])
            turn.give(A(sink[:], tile()[:, 0:8], ACT.Copy), S["rows_spread"])

            act.wait_ge(x_loaded, 16)
            squares(x)
            norm_root(D)
            b_in = v("ab_b_in")
            for j in range(HTL):
                turn.give(A(sgate[:, j, :], tile()[:, 0:T], ACT.Sigmoid, bias=b_in[:, 4 + j:5 + j]), S["glu_gate"])
            for j in range(HTL):
                turn.give(A(rpad[:, j, LK - 1:], tile()[:, 0:T], ACT.Identity, bias=b_in[:, 12 + j:13 + j]),
                          S["rec_in"])
            for j in range(HTL):
                turn.give(A(gin[:, j, :], tile()[:, 0:T], ACT.Gelu_apprx_tanh, bias=b_in[:, 8 + j:9 + j]),
                          S["gelu_in"])
            for c in range(2):
                ada_out(0, c)
            for j in range(HTL):
                turn.give(A(th[:, j, :], tile()[:, 0:T], ACT.Sigmoid, bias=v("b_a")[:, j:j + 1]), S["lru_gate"])
                turn.give(A(bx[:, j, :], tile()[:, 0:T], ACT.Sigmoid, bias=v("b_x")[:, j:j + 1]), S["lru_gate"])
            turn.take(S["lam_abs"])
            turn.give(A(lamt[:, 4:8], lamt[:, 0:4], ACT.Exp, scale=-1.0), achain)
            turn.own(achain)
            turn.give(A(lamt[:, 8:12], lamt[:, 4:8], ACT.Ln, bias=1.0), S["lam_ln"])
            turn.take(S["lam_rate"])
            turn.own(S["lru_gate"])
            for j in range(HTL):
                last = A(th[:, j, :], th[:, j, :], ACT.Tanh, scale=lamt[:, 16 + j:17 + j])
                turn.give(last, S["lru_tanh"])
            turn.own(S["lru_tanh"])
            turn.give(A(den_a[:], th[:], ACT.Sqrt), S["lru_root"])
            for c in range(2, 12):
                ada_out(0, c)
            squares(cv, S["ln_centred"], HTL)
            norm_root(HALF)
            for j in range(HTL):
                turn.take(S["ln_normed"])
                turn.give(A(sgate[:, j, :], cv[:, j, :], ACT.Sigmoid), S["ln_sigmoid"])

            def project_norm():
                for m in range(KT):
                    turn.give(A(h[:, m, :], tile()[:, 0:T], ACT.Copy), S["proj_copied"])
                    turn.own(S["proj_copied"])
                    turn.give(A(sq[:, m, :], h[:, m, :], ACT.Square), S["squares"])
                norm_root(D)

            def ffn():
                squares(x, S["x_ready"])
                norm_root(D)
                for m in range(FT):
                    turn.give(A(sgt[:, m % 2, :], tile()[:, 0:T], ACT.Sigmoid), S["ffn_sig"])
                project_norm()

            project_norm()
            ffn()

            squares(x, S["x_ready"])
            norm_root(D)
            mb = v("ml_b")
            for j in range(HTL):
                turn.give(A(q_m[:, j, :], tile()[:, 0:T], ACT.Identity, bias=mb[:, j:j + 1]), S["mq"])
            turn.take(S["kb_scaled"])
            for j in range(HTL):
                turn.give(A(k_m[:, j, :], tile()[:, 0:T], ACT.Identity, bias=lamt[:, 20 + j:21 + j], scale=0.125),
                          S["mk"])
            for j in range(KT):
                turn.give(A(so[:, j, :], tile()[:, 0:T], ACT.Sigmoid, bias=mb[:, 8 + j:9 + j]), S["mo"])
            turn.take(S["f_abs"])
            turn.give(A(ghead[:, 2, :], ghead[:, 2, :], ACT.Exp, scale=-1.0), achain)
            turn.own(achain)
            turn.give(A(ghead[:, 2, :], ghead[:, 2, :], ACT.Ln, bias=1.0), S["f_ln"])
            for c in range(2):
                for t in range(TT):
                    turn.give(A(v_m[:, t, c * CH:(c + 1) * CH], tile(), ACT.Copy), S["mv"])
            for c in range(4):
                ada_out(1, c)
            turn.take(S["gate_m"])
            turn.give(A(ghead[:, 3, :], ghead[:, 3, :], ACT.Exp, scale=-1.0), S["gate_expm"])

            def decay(n):
                turn.take(S["exponents"])
                turn.give(A(dexp[:, n % 2, :], darg[:, n % 2, :], ACT.Exp, scale=-1.0), S["decays"])

            decay(0)
            for n in range(HEADS):
                if n + 1 < HEADS:
                    decay(n + 1)
                ada_out(1, 4 + n)
                turn.give(A(absd[:, n % 2, :], tile()[:, 0:T], ACT.Abs), S["absden"])
            squares(y_m, S["head_out"])
            for n in range(HEADS):
                turn.give(A(sq[:, n, :], tile()[:, 0:T], ACT.Sqrt, bias=eps[:], scale=1.0 / P), S["head_roots"])
            project_norm()
            ffn()

            turn.own(S["roots"])
            act.dma_start(ctxr[:], a["ctx"]).then_inc(ctx_loaded, 16)
            act.wait_ge(ctx_loaded, 16)
            squares(ctxr)
            norm_root(D, root_c)
            squares(x, S["x_ready"])
            norm_root(D)
            for s in range(2):
                turn.give(A(kraw[:, s, :], tile()[:, 0:T], ACT.Copy), S["kraw_ready"])
            turn.give(A(v_a[:], tile().rearrange("p (a b) -> p a b", a=4), ACT.Copy), S["vals"])
            for j in range(HTL):
                turn.give(A(q_a[:, j, :], tile()[:, 0:T], ACT.Copy), S["qraw_ready"])
            for j in range(HTL):
                turn.give(A(u_a[:, j, :], tile()[:, 0:T], ACT.Gelu), S["u_gelu"])
            for t in range(TT):
                turn.give(A(z_a[:, t, :], tile(), ACT.Gelu), S["z_gelu"])
            for kv in range(2):
                turn.give(A(kd[:, kv, 0:T], tile()[:, 0:T], ACT.Copy), S["k_ctx"])
            turn.take(S["z_centred"])
            for t in range(TT):
                turn.give(A(z_a[:, t, :], zc[:, t, :], ACT.Square, accum_out=small[:, 4 + t:5 + t]), S["z_sq"])
            turn.own(S["z_sq"])
            turn.give(A(small[:, 6:8], small[:, 4:6], ACT.Sqrt, bias=eps[:], scale=1.0 / HALF), S["z_root"])

            def att_exp(i):
                turn.take(S["maxima"])
                turn.give(A(pexp[:, i % 2, :], sm[:, i % 2, :], ACT.Exp, bias=small[:, 10 + i % 2:11 + i % 2],
                            accum_out=small[:, 12 + i % 2:13 + i % 2]), achain)
                turn.own(achain)
                turn.give(A(small[:, 14 + i % 2:15 + i % 2], sink[:, i // 2:i // 2 + 1], ACT.Exp,
                            bias=small[:, 10 + i % 2:11 + i % 2]), S["exps"])

            att_exp(0)
            for i in range(2 * HEADS):
                if i + 1 < 2 * HEADS:
                    att_exp(i + 1)
                turn.give(A(pt[:, i % 2, :], tile(), ACT.Copy), S["pt_ready"])
                if i % 4 == 3:
                    turn.give(A(mix[:, i // 4, :], tile()[:, 0:T], ACT.Copy), S["att_out"])

            def latent_norm():
                squares(x, S["x_added"])
                norm_root(D)

            latent_norm()

            def experts(l):
                e_ = E[l]
                for t in range(TT):
                    turn.take(S["router_max"])
                    turn.give(A(rt[:, 5, 0:4], lg[:, t, 0:4], ACT.Exp, bias=small[:, 20:21],
                                accum_out=small[:, 21:22]), S["router_exp"])
                    turn.take(S["router_gap"])
                    turn.give(A(small[:, 23:24], small[:, 22:23], ACT.Exp), S["router_gexp"])
                with act.Fori(0, NEXP // 2) as i:
                    for e in range(2):
                        act.wait_ge(e_["row_full"], 2 * i + e + 1)
                        A(gb[:, e, :], ps[:, 3, 0:T], ACT.Copy).then_inc(e_["row_copied"], 1)
                        for m in range(HTL):
                            act.wait_ge(e_["gate_full"], 8 * i + 4 * e + m + 1)
                            A(esg[:, m % 2, :], ps[:, 2 * (m % 2), 0:T], ACT.Sigmoid).then_inc(e_["gate_sig"], 1)
                latent_norm()

            experts(0)
            for c in range(6):
                if c in (0, 2):
                    for j in range(HTL):
                        turn.give(A(cg[:, 2 * c + j, :], tile()[:, 0:T], ACT.Copy), S["cgate"])
                elif c >= 4:
                    for j in range(HTL):
                        turn.give(A(bg[:, 4 * (c - 4) + j, :], tile()[:, 0:T], ACT.Copy), S["bgate"])
            latent_norm()
            experts(1)

        @block.vector
        def _(dve):
            turn = Turns(dve)
            where = iter(bank_of[tiles_dve])
            gates = iter(gate_bank)
            V = nc.vector

            def step(instruction, signal=vchain):
                turn.give(instruction, signal)
                turn.own(signal)

            def tile():
                turn.take(tiles_dve)
                return ps[:, next(where), :]

            def stt(out_, in0, scalar, in1, op0, op1):
                return V.scalar_tensor_tensor(out=out_, in0=in0, scalar=scalar, in1=in1, op0=op0, op1=op1)

            def inverse_root(src=root):
                turn.take(S["roots"])
                step(V.reciprocal(rstd[:], src[:]))

            def pre_norm(g):
                inverse_root()
                for k in range(KT):
                    step(stt(h[:, k, :], x[:, k, :], g[:, k:k + 1], rstd[:], ALU.mult, ALU.mult), S["h_ready"])

            def post_norm(g):
                inverse_root()
                for k in range(KT):
                    step(stt(tmp[:, k % 2, :], h[:, k, :], g[:, k:k + 1], rstd[:], ALU.mult, ALU.mult))
                    step(V.tensor_tensor(x[:, k, :], x[:, k, :], tmp[:, k % 2, :], ALU.add), S["x_ready"])

            def gain(name, l):
                return v(name)[:, 8 * l:8 * l + 8]

            dve.wait_ge(memsets, 6)
            dve.wait_ge(consts_loaded, 16 * 8)
            step(stt(lamt[:, 0:4], v("lam"), -1.0, v("lam"), ALU.mult, ALU.max), S["lam_abs"])
            step(V.tensor_scalar(lamt[:, 20:24], v("ml_b")[:, 4:8], 0.125, None, ALU.mult), S["kb_scaled"])
            turn.take(S["c_sigmoid"])
            step(V.tensor_tensor(silu_c[:], silu_c[:], v("c").rearrange("p (a b) -> p a b", b=2), ALU.mult),
                 S["silu_c"])

            dve.wait_ge(x_loaded, 16)
            pre_norm(gain("pre_mix_g", 0))
            b_in = v("ab_b_in")
            for j in range(HTL):
                turn.take(S["glu_gate"])
                step(stt(cpad[:, j, CK - 1:], tile()[:, 0:T], b_in[:, j:j + 1], sgate[:, j, :], ALU.add, ALU.mult),
                     S["glu"])

            def conv(dst, src, w, bias, taps, done):
                for k in range(taps):
                    for j in range(HTL):
                        s, wk = src[:, j, k:k + T], w[:, j * taps + k:j * taps + k + 1]
                        if k == 0:
                            turn.give(V.tensor_scalar(dst[:, j, :], s, wk, bias[:, j:j + 1], ALU.mult, ALU.add), vchain)
                            continue
                        turn.own(vchain, HTL - 1)
                        last = stt(dst[:, j, :], s, wk, dst[:, j, :], ALU.mult, ALU.add)
                        turn.give(last, vchain)
                turn.own(vchain)
                for j in range(HTL):
                    turn.give(V.tensor_copy(small[:, 40 + j:41 + j], dst[:, j, 0:1]), done)

            turn.take(S["rec_in"], HTL)
            conv(xr, rpad, v("lru_w"), v("lru_b"), LK, S["lru_conv"])
            turn.take(S["lam_ln"])
            step(stt(lamt[:, 12:16], v("lam"), -1.0, zeros[:, 0:4], ALU.mult, ALU.max))
            step(V.tensor_tensor(lamt[:, 12:16], lamt[:, 12:16], lamt[:, 8:12], ALU.add))
            step(V.tensor_scalar(lamt[:, 16:20], lamt[:, 12:16], LRU_C / 2, None, ALU.mult), S["lam_rate"])
            conv(cv, cpad, v("conf_w"), v("conf_b"), CK, S["conf_conv"])
            turn.take(S["lru_gate"], 2 * HTL)
            turn.take(S["lru_tanh"], HTL)
            u = ymix[:, HTL:KT, :]
            step(V.tensor_tensor(bx[:], bx[:], xr[:], ALU.mult))
            step(V.tensor_scalar(u, th[:], 1.0, None, ALU.add))
            step(V.reciprocal(u, u))
            turn.take(S["lru_root"])
            step(V.tensor_tensor(den_a[:], den_a[:], u, ALU.mult))
            step(stt(bx[:], bx[:], 2.0, den_a[:], ALU.mult, ALU.mult))
            step(V.tensor_scalar(th[:], u, 2.0, -1.0, ALU.mult, ALU.add))
            for j in range(HTL):
                turn.give(V.tensor_tensor_scan(den_a[:, j, :], th[:, j, :], bx[:, j, :], 0.0, ALU.mult, ALU.add),
                          vchain)
            turn.own(vchain)
            turn.take(S["gelu_in"], HTL)
            step(V.tensor_tensor(ymix[:, HTL:KT, :], den_a[:], gin[:], ALU.mult))
            step(V.tensor_scalar(tmp[:, 0, :], tile()[:, 0:T], 1.0 / HALF, None, ALU.mult), S["ln_mean"])
            for j in range(HTL):
                step(V.tensor_tensor(cv[:, j, :], cv[:, j, :], tmp[:, 0, :], ALU.subtract), S["ln_centred"])
            inverse_root()
            for j in range(HTL):
                step(stt(cv[:, j, :], cv[:, j, :], v("ln_g")[:, j:j + 1], rstd[:], ALU.mult, ALU.mult))
                step(V.tensor_scalar(cv[:, j, :], cv[:, j, :], v("ln_b")[:, j:j + 1], None, ALU.add), S["ln_normed"])
            for j in range(HTL):
                turn.take(S["ln_sigmoid"])
                step(V.tensor_tensor(ymix[:, j, :], cv[:, j, :], sgate[:, j, :], ALU.mult), S["mixed"])

            def ffn(l):
                post_norm(gain("post_mix_g", l))
                pre_norm(gain("pre_ffn_g", l))
                for m in range(FT):
                    turn.take(S["ffn_sig"])
                    step(V.tensor_tensor(fft[:, m % 2, :], ps[:, next(gates), 0:T], sgt[:, m % 2, :], ALU.mult),
                         S["ffn_gate_read"])
                    step(V.tensor_tensor(ff[:, m, :], tile()[:, 0:T], fft[:, m % 2, :], ALU.mult), S["hidden"])
                post_norm(gain("post_ffn_g", l))

            ffn(0)

            pre_norm(gain("pre_mix_g", 1))
            step(V.tensor_copy(gtok[:], tile()[:, 0:32].rearrange("p (a b) -> p a b", a=TT)), S["gates_tok"])
            step(V.tensor_copy(ghead[:, 0:2, :], tile()[0:8].rearrange("p (a b) -> p a b", a=2)), S["gates_head"])
            step(stt(ghead[:, 2, :], ghead[:, 1, :], -1.0, ghead[:, 1, :], ALU.mult, ALU.max), S["f_abs"])
            turn.take(S["f_ln"])
            step(stt(ghead[:, 1, :], ghead[:, 1, :], 0.0, ghead[:, 2, :], ALU.min, ALU.subtract))
            step(V.tensor_tensor_scan(ghead[:, 3, :], ghead[:, 1, :], zeros[0:8, 0:T], 0.0, ALU.add, ALU.add))
            step(V.tensor_tensor(ghead[:, 0, :], ghead[:, 0, :], ghead[:, 3, :], ALU.subtract), S["gate_a"])
            step(V.tensor_tensor_scan(ghead[:, 2, :], ghead[:, 0, :], ghead[:, 0, :], 0.0, ALU.max, ALU.max))
            step(V.tensor_tensor(ghead[:, 3, :], ghead[:, 3, :], ghead[:, 2, :], ALU.add), S["gate_m"])
            step(V.tensor_copy(acol[:], tile()[:, 0:16].rearrange("p (a b) -> p a b", a=TT)), S["acol_ready"])

            def exponents(n):
                big = tile()
                step(stt(darg[:, n % 2, 0:T], big[:, 0:T], acol[:, 0, n:n + 1], tri, ALU.subtract, ALU.max))
                step(stt(darg[:, n % 2, T:T + P], big[:, P:T], acol[:, 1, n:n + 1], tri[:, 0:P],
                         ALU.subtract, ALU.max), S["exponents"])
                return tile()

            following = exponents(0)
            for n in range(HEADS):
                scores = following
                if n + 1 < HEADS:
                    following = exponents(n + 1)
                turn.take(S["decays"])
                step(V.tensor_tensor(pm[:, n % 2, :], scores[:, 0:384], dexp[:, n % 2, :], ALU.mult), S["weighted"])
                turn.take(S["absden"])
                step(V.tensor_tensor(tmp[:, 0, :], ps[:, 7, T:2 * T], absd[:, n % 2, :], ALU.max), S["den_read"])
                step(V.reciprocal(tmp[:, 1, :], tmp[:, 0, :]))
                step(V.tensor_tensor(y_m[:, n, :], tile()[:, 0:T], tmp[:, 1, :], ALU.mult), S["head_out"])
            turn.take(S["mo"], KT)
            for n in range(HEADS):
                turn.take(S["head_roots"])
                step(V.reciprocal(sq[:, n, :], sq[:, n, :]))
                step(stt(y_m[:, n, :], y_m[:, n, :], v("head_g")[:, n:n + 1], sq[:, n, :], ALU.mult, ALU.mult))
                step(V.tensor_tensor(y_m[:, n, :], y_m[:, n, :], so[:, n, :], ALU.mult), S["mixed"])
            ffn(1)

            turn.take(S["ada_raw"], 24)
            bias = v("b_ada").rearrange("p (l m) -> p l m", l=2)
            for w in range(2):
                step(V.tensor_tensor(ada[:, :, :, w], ada[:, :, :, w], bias, ALU.add))
            for i, (l, part, w, g) in enumerate(((0, 1, 0, "g_norm1"), (0, 1, 1, "g_norm1"), (0, 4, 0, "g_norm2"),
                                                 (1, 1, 0, "g_norm1"), (1, 4, 0, "g_norm2"))):
                step(stt(scale_g[:, i, :], ada[:, l, 8 * part:8 * part + 8, w], 1.0, gain(g, l), ALU.add, ALU.mult))

            def modulated_norm(dst, src, which, l, part, w, ready, from_root=root):
                inverse_root(from_root)
                for k in range(KT):
                    step(stt(tmp[:, k % 2, :], src[:, k, :], scale_g[:, which, k:k + 1], rstd[:], ALU.mult, ALU.mult))
                    step(V.tensor_scalar(dst[:, k, :], tmp[:, k % 2, :], ada[:, l, 8 * part + k, w:w + 1], None,
                                         ALU.add), ready)

            modulated_norm(hc, ctxr, 1, 0, 0, 1, S["hc_ready"], root_c)
            modulated_norm(h, x, 0, 0, 0, 0, S["h_ready"])
            for kv in range(2):
                src = tile()
                step(V.tensor_tensor(rope_t[:, 0, :], src[:, 0:T], cos, ALU.mult))
                step(V.tensor_tensor(rope_t[:, 1, :], src[:, T:2 * T], sin, ALU.mult), S["k_rope_read"])
                step(V.tensor_tensor(kd[:, kv, T:2 * T], rope_t[:, 0, :], rope_t[:, 1, :], ALU.add))
            turn.take(S["qraw_ready"], HTL)
            for j in range(HTL):
                step(V.tensor_tensor(rope_t[:, 1, :], tile()[:, 0:T], sin, ALU.mult), S["q_rope_read"])
                step(V.tensor_tensor(rope_t[:, 0, :], q_a[:, j, :], cos, ALU.mult))
                step(V.tensor_tensor(q_a[:, j, :], rope_t[:, 0, :], rope_t[:, 1, :], ALU.add),
                     S["rotated"] if j == HTL - 1 else vchain)
            turn.take(S["z_gelu"], TT)
            for t in range(TT):
                step(V.tensor_reduce(small[:, 0:1], z_a[:, t, :], AX, ALU.add))
                step(V.tensor_scalar(small[:, 1:2], small[:, 0:1], 1.0 / HALF, None, ALU.mult))
                step(V.tensor_scalar(zc[:, t, :], z_a[:, t, :], small[:, 1:2], None, ALU.subtract),
                     S["z_centred"] if t == TT - 1 else vchain)
            turn.take(S["z_root"])
            turn.take(S["z_sq"], TT)
            turn.take(S["rows_spread"], 2)
            step(V.reciprocal(small[:, 8:10], small[:, 6:8]))
            for t in range(TT):
                step(stt(z_a[:, t, :], zc[:, t, :], small[:, 8 + t:9 + t], sgu_g[:], ALU.mult, ALU.mult),
                     S["z_normed"] if t == TT - 1 else vchain)

            def att_max(i):
                n, t, c = i // 2, i % 2, i % 2
                step(stt(sm[:, c, :], tile(), 0.125, window[:, t, :], ALU.mult, ALU.add), S["scores_read"])
                step(V.tensor_reduce(small[:, 16 + c:17 + c], sm[:, c, :], AX, ALU.max))
                step(V.tensor_scalar(small[:, 10 + c:11 + c], small[:, 16 + c:17 + c], sink[:, n:n + 1], -1.0,
                                     ALU.max, ALU.mult), S["maxima"])

            att_max(0)
            for i in range(2 * HEADS):
                if i + 1 < 2 * HEADS:
                    att_max(i + 1)
                c = i % 2
                turn.take(S["exps"])
                step(V.tensor_tensor(small[:, 18 + c:19 + c], small[:, 12 + c:13 + c], small[:, 14 + c:15 + c],
                                     ALU.add))
                step(V.reciprocal(small[:, 18 + c:19 + c], small[:, 18 + c:19 + c]))
                step(V.tensor_scalar(pexp[:, c, :], pexp[:, c, :], small[:, 18 + c:19 + c], None, ALU.mult),
                     S["probs"])
            turn.take(S["u_gelu"], HTL)
            for j in range(HTL):
                step(V.tensor_tensor(mix[:, HTL + j, :], tile()[:, 0:T], u_a[:, j, :], ALU.mult), S["mixed"])

            def add_to_x(src, k, l, part):
                step(stt(x[:, k, :], src, ada[:, l, 8 * part + k, 0:1], x[:, k, :], ALU.mult, ALU.add), S["x_added"])

            def one_hot(dst, values, top, n):
                step(V.tensor_scalar(rt[:, 0, 0:n], values, top, None, ALU.is_equal))
                step(V.tensor_tensor_scan(rt[:, 1, 0:n], rt[:, 0, 0:n], zeros[:, 0:n], 0.0, ALU.add, ALU.add))
                step(stt(dst, rt[:, 1, 0:n], 1.0, rt[:, 0, 0:n], ALU.is_equal, ALU.mult))

            def route(t):
                step(V.tensor_reduce(small[:, 24:25], lg[:, t, 0:NGRP], AX, ALU.max))
                step(V.tensor_scalar(small[:, 20:21], small[:, 24:25], -1.0, None, ALU.mult), S["router_max"])
                one_hot(small[:, 28:32], lg[:, t, 0:NGRP], small[:, 24:25], NGRP)
                step(V.tensor_scalar(small[:, 32:36], small[:, 28:32], 1.0, BIG, ALU.subtract, ALU.mult))
                for g in range(NGRP):
                    s = slice(NGRP + EPG * g, NGRP + EPG * (g + 1))
                    step(V.tensor_scalar(rt[:, 2, EPG * g:EPG * (g + 1)], lg[:, t, s], small[:, 32 + g:33 + g], None,
                                         ALU.add))
                step(V.tensor_reduce(small[:, 25:26], rt[:, 2, :], AX, ALU.max))
                one_hot(rt[:, 3, :], rt[:, 2, :], small[:, 25:26], NEXP)
                step(stt(rt[:, 2, :], rt[:, 3, :], -2.0 * BIG, rt[:, 2, :], ALU.mult, ALU.add))
                step(V.tensor_reduce(small[:, 26:27], rt[:, 2, :], AX, ALU.max))
                one_hot(rt[:, 4, :], rt[:, 2, :], small[:, 26:27], NEXP)
                turn.take(S["router_exp"])
                step(V.tensor_tensor(small[:, 22:23], small[:, 26:27], small[:, 25:26], ALU.subtract),
                     S["router_gap"])
                step(V.reciprocal(small[:, 36:37], small[:, 21:22]))
                turn.take(S["router_gexp"])
                step(V.tensor_scalar(small[:, 37:38], small[:, 23:24], 1.0, None, ALU.add))
                step(V.reciprocal(small[:, 38:39], small[:, 37:38]))
                step(V.tensor_tensor(small[:, 38:39], small[:, 38:39], small[:, 36:37], ALU.mult))
                step(V.tensor_tensor(small[:, 39:40], small[:, 38:39], small[:, 23:24], ALU.mult))
                step(V.tensor_scalar(G[:, t, :], rt[:, 3, :], small[:, 38:39], None, ALU.mult))
                step(stt(G[:, t, :], rt[:, 4, :], small[:, 39:40], G[:, t, :], ALU.mult, ALU.add))

            def experts(l):
                e_ = E[l]
                modulated_norm(h, x, 2 if l == 0 else 4, l, 3, 0, S["h_ready"])
                step(V.tensor_copy(lg[:], tile()[:, 0:TT * NLOG].rearrange("p (a b) -> p a b", a=TT)),
                     S["logits_read"])
                for t in range(TT):
                    route(t)
                V.memset(small[:, 50:51], 0.0).then_inc(e_["gate_freed"], 1)
                V.memset(small[:, 51:52], 0.0).then_inc(e_["gate_freed"], 1)
                V.memset(small[:, 52:53], 0.0).then_inc(e_["up_freed"], 1)
                V.memset(small[:, 53:54], 0.0).then_inc(e_["row_copied"], 1)
                with dve.Fori(0, NEXP // 2) as i:
                    for e in range(2):
                        dve.wait_ge(e_["row_copied"], 2 * i + e + 1)
                        V.tensor_scalar(dg[:, e, 0:P], ident, G[:, 0, bass.ds(2 * i + e, 1)], None, ALU.mult)
                        V.tensor_scalar(dg[:, e, P:T], ident, G[:, 1, bass.ds(2 * i + e, 1)], None,
                                        ALU.mult).then_inc(e_["diag"], 1)
                        for m in range(HTL):
                            dve.wait_ge(e_["gate_sig"], 8 * i + 4 * e + m + 1)
                            V.tensor_tensor(et[:, 0, :], ps[:, 2 * (m % 2), 0:T], esg[:, m % 2, :],
                                            ALU.mult).then_inc(e_["gate_freed"], 1)
                            dve.wait_ge(e_["gate_freed"], 8 * i + 4 * e + m + 3)
                            dve.wait_ge(e_["up_full"], 8 * i + 4 * e + m + 1)
                            V.tensor_tensor(et[:, 1, :], ps[:, 1, 0:T], et[:, 0, :], ALU.mult).then_inc(
                                e_["up_freed"], 1)
                            dve.wait_ge(e_["up_freed"], 8 * i + 4 * e + m + 2)
                            if m == 0:
                                dve.wait_ge(e_["row_copied"], 2 * i + e + 2)
                            V.tensor_tensor(hid[:, e, m * T:(m + 1) * T], et[:, 1, :], gb[:, e, :],
                                            ALU.mult).then_inc(e_["hid_ready"], 1)
                            dve.wait_ge(e_["hid_ready"], 8 * i + 4 * e + m + 1)
                for b in range(4):
                    acc = tile()
                    for i in range(2):
                        add_to_x(acc[:, i * T:(i + 1) * T], 2 * b + i, l, 5)

            for k in range(KT):
                add_to_x(tile()[:, 0:T], k, 0, 2)
            experts(0)

            modulated_norm(h, x, 3, 1, 0, 0, S["h_ready"])
            step(V.memset(ypad[:, :, 0:1], 0.0))
            step(V.memset(ypad[:, :, T + 1:T + 2], 0.0))
            for k in range(KT):
                turn.take(S["cgate"])
                step(V.tensor_tensor(ypad[:, k, 1:T + 1], tile()[:, 0:T], cg[:, k, :], ALU.mult), S["cvalue"])
            cw = v("conv_w")
            for k in range(KT):
                step(V.tensor_scalar(cvo[:, k, :], ypad[:, k, 0:T], cw[:, 3 * k:3 * k + 1], None, ALU.mult))
                for i in (1, 2):
                    step(stt(cvo[:, k, :], ypad[:, k, i:i + T], cw[:, 3 * k + i:3 * k + i + 1], cvo[:, k, :],
                             ALU.mult, ALU.add))
            for k in range(KT):
                turn.take(S["bgate"])
                step(V.tensor_tensor(cvo[:, k, :], cvo[:, k, :], bg[:, k, :], ALU.mult), S["mixed"])
            for k in range(KT):
                add_to_x(tile()[:, 0:T], k, 1, 2)
            experts(1)
            pre_norm(v("g_final"))
            h_count.append(turn.given[S["h_ready"]])

        @block.sync
        def _(sp):
            sp.wait_ge(S["h_ready"], h_count[0])
            sp.dma_start(out, h[:]).then_inc(out_stored, 16)
            sp.wait_ge(out_stored, 16)


def tiled(w):
    import numpy as np
    k, n = w.shape
    w = w.reshape(k // P, P, n // CH, CH)
    return np.ascontiguousarray(w.transpose(2, 1, 0, 3))


def features(vector):
    import numpy as np
    vector = vector.reshape(-1, vector.shape[-1] // P, P)
    return np.ascontiguousarray(vector.transpose(2, 0, 1)).reshape(P, -1)


def shape_constants():
    import numpy as np
    f32 = np.float32
    con = np.zeros((P, NCON), f32)

    def put(name, value):
        con[:value.shape[0], CON[name][0]:CON[name][0] + CON[name][1]] = value.reshape(value.shape[0], -1)

    m, t = np.arange(P), np.arange(T)
    put("ident", np.eye(P, dtype=f32))
    inv = f32(10000.0) ** (-np.arange(16, dtype=f32) / f32(16))
    place = np.where((m % 64 < 32)[:, None], (t // 64)[None, :], (t % 64)[None, :]).astype(f32)
    angle = place * inv[m % 16][:, None]
    put("cos", np.cos(angle).astype(f32))
    put("sin", np.sin(angle).astype(f32))
    partner = np.zeros((P, P), f32)
    partner[np.where(m % 32 < 16, m + 16, m - 16), m] = np.where(m % 32 < 16, -1, 1)
    perm = [partner]
    for kv in range(2):
        both = np.zeros((P, P), f32)
        both[kv * 64 + m % 64, m] = 1
        perm.append(both)
    for kv in range(2):
        pair = np.zeros((P, P), f32)
        for c in range(P):
            pair[:, c] = perm[1 + kv][:, partner[:, c].nonzero()[0][0]] * partner[:, c].sum()
        perm.append(pair)
    put("perm", np.stack(perm, 1))
    put("tri", np.where(t[None, :] >= m[:, None], 0, BIG).astype(f32))
    key = np.arange(2 * T)[None, None, :] - T
    query = m[:, None, None] + P * np.arange(TT)[None, :, None]
    put("window", np.where((key < 0) | (abs(key - query) <= P), 0, -BIG).astype(f32))
    eight = np.arange(8)
    sel8 = np.broadcast_to((eight[:, None] == eight[None, :])[:, :, None], (8, 8, P)).reshape(8, -1)
    selb = (eight[:, None, None] == 2 * np.arange(4)[None, :, None] + m[None, None, :] // 64).reshape(8, -1)
    return con, np.concatenate([sel8, selb], 1).astype(f32)


def kernel(**inputs):
    import numpy as np
    import concourse.bacc as bacc
    from concourse.bass_utils import run_bass_kernel_spmd as run

    g = {n: np.asarray(w) for n, w in inputs.items()}
    arrays = {}

    def feature_major(w):
        return np.ascontiguousarray(w.reshape(T, KT, P).transpose(2, 1, 0))

    arrays["x"] = feature_major(g["x"])
    arrays["ctx"] = feature_major(g["ctx_2"])
    arrays["ab_w_in"] = tiled(g["ab_w_in"][0])
    arrays["ab_w_out"] = tiled(g["ab_w_out"][0])
    arrays["ml_w_in"] = tiled(g["ml_w_in"][0][:, :3072])
    arrays["ml_w_out"] = tiled(g["ml_w_out"][0])

    def columns(w):
        pad = np.zeros((w.shape[0], 6 * CH), w.dtype)
        pad[:, :DFF] = w
        return tiled(pad)

    arrays["w_ff_gate"] = np.stack([columns(w) for w in g["ffn_w_gate"]])
    arrays["w_ff_up"] = np.stack([columns(w) for w in g["ffn_w_up"]])
    arrays["w_ff_down"] = np.stack([tiled(w) for w in g["ffn_w_down"]])
    arrays["w_ada"] = np.stack([tiled(w) for w in g["w_ada_2"]])
    even = g["w_in_even_2"][0]
    arrays["w_even"] = np.stack([tiled(even[:, c:c + CH])[0] for c in (0, 768, 1280)])
    arrays["w_even_kv"] = np.ascontiguousarray(even[:, 512:768].reshape(KT, P, 256).transpose(1, 0, 2))
    arrays["w_even_out"] = tiled(g["w_out_even_2"][0])
    arrays["w_odd"] = tiled(g["w_in_odd_2"][0])
    arrays["w_odd_out"] = tiled(g["w_out_odd_2"][0])
    for name in ("gate", "up"):
        w = g[f"w_{name}_2"].reshape(2, NEXP, KT, P, EH)
        arrays[f"w_{name}"] = np.ascontiguousarray(w.transpose(0, 1, 3, 2, 4)).reshape(2, NEXP, P, SLOT)
    w = g["w_down_2"].reshape(2, NEXP, HTL, P, D)
    arrays["w_down"] = np.ascontiguousarray(w.transpose(0, 1, 3, 2, 4)).reshape(2, NEXP, P, SLOT)

    mb = g["ml_b_in"][0]
    parts = dict(
        pre_mix_g=features(g["pre_mix_g"]), post_mix_g=features(g["post_mix_g"]),
        pre_ffn_g=features(g["pre_ffn_g"]), post_ffn_g=features(g["post_ffn_g"]),
        ab_b_in=features(g["ab_b_in"]),
        conf_w=np.ascontiguousarray(g["conf_conv_w"][0].reshape(CK, HTL, P).transpose(2, 1, 0)).reshape(P, -1),
        conf_b=features(g["conf_conv_b"]), ln_g=features(g["conf_ln_g"]), ln_b=features(g["conf_ln_b"]),
        lru_w=np.ascontiguousarray(g["lru_conv_w"][0].reshape(LK, HTL, P).transpose(2, 1, 0)).reshape(P, -1),
        lru_b=features(g["lru_conv_b"]), b_a=features(g["lru_b_a"].reshape(1, HALF)),
        b_x=features(g["lru_b_x"].reshape(1, HALF)), lam=features(g["lru_lambda"]),
        ml_b=features(np.concatenate([mb[0:1024], mb[2048:3072]])[None]), head_g=features(g["ml_head_g"]),
        c=np.ascontiguousarray(np.stack([g["c_2"][0], g["c_ctx_2"]]).reshape(2, KT, P).transpose(2, 1, 0)
                               ).reshape(P, -1),
        b_ada=features(g["b_ada_2"]), g_norm1=features(g["g_norm1_2"]), g_norm2=features(g["g_norm2_2"]),
        g_final=features(g["g_final_2"][None]),
        conv_w=np.ascontiguousarray(g["conv_w_2"][0].reshape(3, KT, P).transpose(2, 1, 0)).reshape(P, -1))
    arrays["vec"] = np.concatenate([parts[n] for n, _ in VEC_SIZES], 1)
    arrays["con"], arrays["sel"] = shape_constants()
    rows = dict(v_b=mb[1024:2048], gate_b=mb[3072:3088],
                router_b=np.concatenate([g["b_router_group_2"], g["b_router_expert_2"]], 1).reshape(-1),
                g_sgu=g["g_sgu_2"][0], sink=g["attn_sink_2"][0])
    arrays["row"] = np.concatenate([rows[n] for n, _ in ROW_SIZES])[None]
    arrays["gate_w"] = np.ascontiguousarray(g["ml_w_in"][0][:, 3072:].reshape(KT, P, 16).transpose(1, 0, 2))
    router = np.concatenate([g["w_router_group_2"], g["w_router_expert_2"]], 2)
    arrays["router_w"] = np.ascontiguousarray(router.reshape(2, KT, P, NLOG).transpose(2, 0, 1, 3))
    arrays["w_sp"] = np.ascontiguousarray(g["w_spatial_2"][0].transpose(2, 0, 1))
    arrays["b_sp"] = np.ascontiguousarray(g["b_spatial_2"][0])
    arrays["lru_w"] = np.ascontiguousarray(np.stack([g["lru_w_a"][0], g["lru_w_x"][0]]).reshape(
        2, HTL, 2, 64, 64).transpose(0, 2, 3, 1, 4))

    nc = bacc.Bacc("TRN2", target_bir_lowering=False, num_devices=1)
    handles = {n: nc.dram_tensor(f"in_{n}", w.shape, F32, kind="ExternalInput").ap() for n, w in arrays.items()}
    out = nc.dram_tensor("out", (P, KT, T), F32, kind="ExternalOutput").ap()
    build(nc, handles, out)
    result = run(nc, [{f"in_{n}": w for n, w in arrays.items()}], core_ids=[0])
    got = result.results[0]["out"]
    return np.ascontiguousarray(got.transpose(2, 1, 0).reshape(1, T, D))
```

```python
from contextlib import ExitStack

import concourse.bass as bass
from concourse import mybir

F32 = mybir.dt.float32
ALU = mybir.AluOpType
ACT = mybir.ActivationFunctionType
AX = mybir.AxisListType.X

P = 128
D = 1024
KT = D // P
T = 256
TT = T // P
DFF = 2816
FT = DFF // P
CH = 512
RING = 6
SLOT = KT * CH
EPS = 1e-6
WORK = 12080
HALF = 512
HTL = HALF // P
CK = 31
LK = 4
PE_CONV = 2
TAPS = 16
HEADS = 8
NEXP = 32
NGRP = 4
EPG = NEXP // NGRP
NLOG = NGRP + NEXP
EH = 512
CAP = 64
PAIR = 2 * CAP
NE2 = NEXP + 2
BIG = 1e30
LRU_C = 8.0

VEC_SIZES = [("pre_mix_g", 16), ("post_mix_g", 16), ("pre_ffn_g", 16), ("post_ffn_g", 16), ("ab_b_in", 16),
             ("conf_w", 4 * CK), ("conf_b", 4), ("ln_g", 4), ("ln_b", 4), ("lru_w", 4 * LK), ("lru_b", 4),
             ("b_a", 4), ("b_x", 4), ("lam", 4), ("ml_b", 16), ("head_g", 8), ("c", 16), ("b_ada", 96),
             ("g_norm1", 16), ("g_norm2", 16), ("g_final", 8), ("conv_w", 8 * 3)]
VEC = {}
_at = 0
for _n, _s in VEC_SIZES:
    VEC[_n] = (_at, _s)
    _at += _s
NVEC = _at
CONST_SIZES = [("ident", P), ("cos", T), ("sin", T), ("perm", 5 * P), ("tri", T), ("window", TT * 2 * T), ("below", P), ("iota", CAP)]
CON = {}
_at = 0
for _n, _s in CONST_SIZES:
    CON[_n] = (_at, _s)
    _at += _s
NCON = _at
ROW_SIZES = [("v_b", D), ("gate_b", 16), ("router_b", 2 * NLOG), ("g_sgu", HALF), ("sink", 8)]
ROW = {}
_at = 0
for _n, _s in ROW_SIZES:
    ROW[_n] = (_at, _s)
    _at += _s
NROW = _at
SELS = (8 + 4) * P


class Turns:

    def __init__(self, engine):
        self.engine, self.given, self.taken = engine, {}, {}

    def give(self, instruction, sem):
        instruction.then_inc(sem, 1)
        self.given[sem] = self.given.get(sem, 0) + 1

    def take(self, sem, n=1):
        self.taken[sem] = self.taken.get(sem, 0) + n
        self.engine.wait_ge(sem, self.taken[sem])

    def own(self, sem, but=0):
        if self.given[sem] > but:
            self.engine.wait_ge(sem, self.given[sem] - but)


def build(nc, a, out):
    with ExitStack() as ctx:
        def sb(name, shape):
            return ctx.enter_context(nc.sbuf_tensor(name, shape, F32))

        def sem(name):
            return ctx.enter_context(nc.semaphore(name))

        ring = sb("ring", [P, RING, SLOT])
        x = sb("x", [P, KT, T])
        h = sb("h", [P, KT, T])
        sq = sb("sq", [P, KT, T])
        work = sb("work", [P, WORK])
        vec = sb("vec", [P, NVEC])
        con = sb("con", [P, NCON])
        misc = sb("misc", [33, NROW])
        ones = sb("ones", [P, P])
        zeros = sb("zeros", [P, T])
        bd = sb("bd", [P, 2, HTL, P])
        gw = sb("gw", [P, KT, 16])
        rw = sb("rw", [P, 2, KT, NLOG])
        wsp = sb("wsp", [P, HEADS, P])
        bsp = sb("bsp", [HEADS, P])
        sgu_g = sb("sgu_g", [P, HALF])
        sink = sb("sink", [P, 8])
        silu_c = sb("silu_c", [P, KT, 2])
        ada = sb("ada", [P, 2, 48, 2])
        scale_g = sb("scale_g", [P, 5, KT])
        rstd = sb("rstd", [P, T])
        root = sb("root", [P, T])
        root_c = sb("root_c", [P, T])
        eps = sb("eps", [P, 1])
        small = sb("small", [P, 64])
        lamt = sb("lamt", [P, 32])
        tmp = sb("tmp", [P, 2, T])
        crowd = ctx.enter_context(nc.sbuf_tensor("crowd", [P, 1], mybir.dt.int32))
        ps = ctx.enter_context(nc.psum_tensor("ps", [P, 8, 512], F32))

        def v(name):
            return vec[:, VEC[name][0]:VEC[name][0] + VEC[name][1]]

        def cst(name, n=P):
            return con[0:n, CON[name][0]:CON[name][0] + CON[name][1]]

        def rowv(name):
            return misc[32:33, ROW[name][0]:ROW[name][0] + ROW[name][1]]

        def region(at, *shape, n=P):
            size = 1
            for s in shape:
                size *= s
            assert at + size <= WORK
            w = work[0:n, at:at + size]
            if len(shape) == 2:
                return w.rearrange("p (a b) -> p a b", a=shape[0])
            return w

        ident = cst("ident")
        cos, sin = cst("cos"), cst("sin")
        perm = cst("perm").rearrange("p (a b) -> p a b", a=5)
        tri = cst("tri")
        window = cst("window").rearrange("p (a b) -> p a b", a=TT)
        sel8 = misc[0:8, 0:8 * P].rearrange("p (a b) -> p a b", a=8)
        selb = misc[0:8, 8 * P:SELS].rearrange("p (a b) -> p a b", a=4)
        ones_row = ones[32:33, :]

        sgate = region(0, HTL, T)
        cpad = region(1024, HTL, CK - 1 + T)
        rpad = region(2168, HTL, LK - 1 + T)
        gin = region(3204, HTL, T)
        xr = region(4228, HTL, T)
        th = region(5252, HTL, T)
        den_a = region(6276, HTL, T)
        bx = region(7300, HTL, T)
        cv = region(8324, HTL, T)
        ymix = region(9348, KT, T)
        taps = sq[:].rearrange("p a b -> p (a b)").rearrange("p (a b) -> p a b", a=TAPS)
        ff = region(0, FT, T)
        made = region(FT * T + 4 * T, 2, 2 * 512).rearrange("p a (w c) -> p a w c", w=2)
        sgt = region(FT * T, 2, T)
        fft = region(FT * T + 2 * T, 2, T)
        q_m = region(0, HTL, T)
        k_m = region(1024, HTL, T)
        v_m = region(2048, TT, D)
        so = region(4096, KT, T)
        y_m = region(6144, KT, T)
        darg = region(8192, 2, 384)
        dexp = region(8960, 2, 384)
        pm = region(9728, 2, 384)
        absd = region(10496, 2, T)
        gtok = region(11008, TT, 16)
        acol = region(11040, TT, 8)
        ghead = region(11056, 4, T, n=8)
        ctxr = region(0, KT, T)
        hc = region(2048, KT, T)
        q_a = region(0, HTL, T)
        u_a = region(1024, HTL, T)
        z_a = region(2048, TT, HALF)
        zc = region(3072, TT, HALF)
        kd = region(4096, 2, 2 * T)
        v_a = region(5120, 4, P)
        kraw = region(5632, 2, T)
        rope_t = region(6144, 2, T)
        mix = region(6656, KT, T)
        sm = region(8704, 2, 2 * T)
        pt = region(9728, 2, 2 * T)
        pexp = region(10752, 2, 2 * T)
        bg = region(0, KT, T)
        cg = region(2048, KT, T)
        ypad = region(4096, KT, T + 2)
        cvo = region(6160, KT, T)
        lg = region(0, TT, NLOG)
        G = region(72, TT, NE2)
        rt = region(140, 6, NEXP)
        chosen = region(332, TT, NE2)
        place = region(400, TT, NE2)
        hid = region(512, 2, HTL * T)
        esg = region(2560, 2, T)
        et = region(3072, 2, T)
        dg = region(3584, 2, T)
        gb = region(4096, 2, T)
        xg = region(512, KT, PAIR)
        yt = region(2560, D)
        hs = region(1536, EH)
        hg = region(3584, HTL * PAIR)
        sg = region(4096, EH)
        eg = region(4608, EH)
        pick = region(5120, TT, PAIR)
        weigh = region(5376, TT, PAIR)
        spread = region(5632, T)
        htok = region(8192, TT, D)
        below = cst("below")
        iota = cst("iota")

        consts_loaded = sem("consts_loaded")
        x_loaded = sem("x_loaded")
        ctx_loaded = sem("ctx_loaded")
        blocks_loaded = sem("blocks_loaded")
        slot_loaded = [sem(f"slot{s}_loaded") for s in range(RING)]
        tiles_act = sem("tiles_for_act")
        tiles_dve = sem("tiles_for_dve")
        memsets = sem("memsets_done")
        vchain = sem("vector_step_done")
        achain = sem("scalar_step_done")
        down_part = sem("down_part_done")
        out_stored = sem("out_stored")
        names = ("rows_spread c_sigmoid silu_c ada_raw squares roots x_ready x_added h_ready hc_ready glu_gate glu "
                 "rec_in gelu_in lru_conv ada_made lru_gate lam_abs lam_ln lam_rate lru_tanh lru_root conf_conv tap_ready taps_used tiles_convolved ln_mean "
                 "ln_centred ln_normed ln_sigmoid mixed proj_copied ffn_sig ffn_gate_read hidden kb_scaled mq mk mo mv "
                 "gates_tok gates_head f_abs f_ln gate_a gate_m gate_expm acol_ready exponents decays weighted absden "
                 "den_read head_out head_roots kraw_ready vals qraw_ready u_gelu z_gelu z_centred z_sq z_root z_normed "
                 "k_ctx k_rope_read q_rope_read rotated scores_read maxima exps probs pt_ready att_out logits_read "
                 "router_max router_exp router_done router_gap router_gexp cgate cvalue bgate "
                 "htok_ready chosen_ready crowd_ready").split()
        S = {n: sem(n) for n in names}
        layer_names = ("diag row_full row_copied gate_full gate_sig gate_freed up_full up_freed hid_ready "
                       "down_done masks_ready weights_turned spread_ready gathered xg_ready gated half_done hid_turned hg_ready yt_ready").split()
        E = [{n: sem(f"expert_{n}_{l}") for n in layer_names} for l in range(2)]

        chunks = []

        def chunk(src, nk=KT, cols=CH):
            chunks.append((src, nk, cols))

        for c in (1, 0, 3, 2):
            chunk(a["ab_w_in"][c])
        for c in range(2):
            chunk(a["ab_w_out"][c])

        ada_chunks = []

        def ffn_chunks(l):
            for c in range(6):
                n = min(CH, DFF - c * CH)
                chunk(a["w_ff_gate"][l, c, :, :, 0:n], cols=n)
                chunk(a["w_ff_up"][l, c, :, :, 0:n], cols=n)
                for i in range(2):
                    ada_chunks.append(len(chunks))
                    chunk(a["w_ada"][l, 2 * c + i])
            for c in range(2):
                for k0 in range(0, FT, KT):
                    nk = min(KT, FT - k0)
                    chunk(a["w_ff_down"][l, c, :, k0:k0 + nk, :], nk=nk)

        ffn_chunks(0)
        for c in (0, 1, 4, 5, 2, 3):
            chunk(a["ml_w_in"][c])
        for c in range(2):
            chunk(a["ml_w_out"][c])
        ffn_chunks(1)
        chunk(a["w_even_kv"], cols=256)
        for c in range(3):
            chunk(a["w_even"][c])
        for c in range(2):
            chunk(a["w_even_out"][c])
        moe_first = [len(chunks)]
        for n in range(3 * NEXP):
            chunk(None)
        for c in (2, 4, 3, 5, 0, 1):
            chunk(a["w_odd"][c])
        for c in range(2):
            chunk(a["w_odd_out"][c])
        moe_first.append(len(chunks))
        for n in range(3 * NEXP):
            chunk(None)
        released = {}

        def conditions(l, c):
            return 2 if l == 0 and c < 4 else 1

        bank_of = {tiles_act: [], tiles_dve: []}
        h_count = []
        gate_bank = []

        block = ctx.enter_context(nc.Block())

        @block.tensor
        def _(pe):
            turn = Turns(pe)
            freed = {}
            owner = [None] * 8
            made_so_far = [0]
            state = {"chunk": 0, "bank": 0, "stat": 0}
            mm = nc.tensor.matmul

            def open_bank(b):
                if owner[b] is not None:
                    pe.wait_ge(*owner[b])

            def close_bank(b, last, full, free, reads=1):
                turn.give(last, full)
                bank_of[full].append(b)
                freed[free] = freed.get(free, 0) + reads
                owner[b] = (free, freed[free])

            def next_bank():
                state["bank"] = (state["bank"] + 1) % 4
                open_bank(state["bank"])
                return state["bank"]

            def stat_bank():
                state["stat"] ^= 1
                open_bank(4 + state["stat"])
                return 4 + state["stat"]

            def next_chunk():
                n = state["chunk"]
                state["chunk"] += 1
                pe.wait_ge(slot_loaded[n % RING], 16 * (n // RING + 1))
                _, nk, cols = chunks[n]
                return n, ring[:, n % RING, 0:nk * cols].rearrange("p (k c) -> p k c", k=nk)

            def release(n, full):
                released[n] = (full, turn.given[full])

            def product(w, m, rhs, full, free, ready=None, nready=KT):
                b = next_bank()
                nk = rhs.shape[1]
                for k in range(nk):
                    if ready is not None and k < nready:
                        turn.take(ready)
                    last = mm(ps[:, b, 0:T], w[:, k, m * P:(m + 1) * P], rhs[:, k, :],
                              start=(k == 0), stop=(k == nk - 1))
                close_bank(b, last, full, free)
                return b

            def dense(rhs, full, free, ready=None, nready=KT):
                n, w = next_chunk()
                for m in range(w.shape[2] // P):
                    product(w, m, rhs, full, free, ready, nready)
                    ready = None
                release(n, full)

            def stats(n=KT):
                b = stat_bank()
                for k in range(n):
                    turn.take(S["squares"])
                    last = mm(ps[:, b, 0:T], ones[:], sq[:, k, :], start=(k == 0), stop=(k == n - 1))
                close_bank(b, last, tiles_act, S["roots"])

            def ada_sums(l, c):
                for w in range(conditions(l, c)):
                    turn.take(S["ada_made"])
                    b = stat_bank()
                    for m in range(4):
                        last = mm(ps[:, b, 2 * m:2 * m + 2], made[:, c % 2, w, m * P:(m + 1) * P], ones[:, 0:2],
                                  start=True, stop=True)
                    close_bank(b, last, tiles_act, S["ada_raw"])

            pe.wait_ge(consts_loaded, 16 * 8)
            pe.wait_ge(memsets, 6)
            b = stat_bank()
            close_bank(b, mm(ps[:, b, 0:HALF], ones_row, rowv("g_sgu"), start=True, stop=True),
                       tiles_act, S["rows_spread"])
            b = stat_bank()
            close_bank(b, mm(ps[:, b, 0:8], ones_row, rowv("sink"), start=True, stop=True),
                       tiles_act, S["rows_spread"])

            stats()
            dense(h, tiles_act, S["glu_gate"], S["h_ready"])
            dense(h, tiles_dve, S["glu"])
            dense(h, tiles_act, S["rec_in"])
            dense(h, tiles_act, S["gelu_in"])
            pe.wait_ge(blocks_loaded, 64)
            for j in range(HTL):
                turn.take(S["lru_conv"])
                for g in range(2):
                    b = next_bank()
                    close_bank(b, mm(ps[:, b, 0:T], bd[:, g, j, :], xr[:, j, :], start=True, stop=True),
                               tiles_act, S["lru_gate"])
            turn.take(S["glu"], HTL)
            for n in range(PE_CONV * CK):
                j, k = HTL - PE_CONV + n // CK, n % CK
                if k == 0:
                    b = next_bank()
                turn.take(S["tap_ready"])
                last = mm(ps[:, b, 0:T], taps[:, n % TAPS, :], cpad[:, j, k:k + T], start=(k == 0), stop=(k == CK - 1))
                if k == CK - 1:
                    close_bank(b, last, tiles_act, S["tiles_convolved"])
                elif n % (TAPS // 2) == TAPS // 2 - 1:
                    turn.give(last, S["taps_used"])
            b = stat_bank()
            for j in range(HTL):
                turn.take(S["conf_conv"] if j < HTL - PE_CONV else S["tiles_convolved"])
                last = mm(ps[:, b, 0:T], ones[:], cv[:, j, :], start=(j == 0), stop=(j == HTL - 1))
            close_bank(b, last, tiles_dve, S["ln_mean"])
            stats(HTL)

            def project_norm(src, nready):
                dense(src, tiles_act, S["proj_copied"], S["mixed"], nready)
                dense(src, tiles_act, S["proj_copied"])
                stats()

            project_norm(ymix, HTL)

            def ffn(l):
                stats()
                ready = S["h_ready"]
                for c in range(6):
                    ng, wg = next_chunk()
                    nu, wu = next_chunk()
                    for m in range(wg.shape[2] // P):
                        gate_bank.append(product(wg, m, h, tiles_act, S["ffn_gate_read"], ready))
                        ready = None
                        product(wu, m, h, tiles_dve, S["hidden"])
                        if c and m == 0:
                            ada_sums(l, 2 * c - 2)
                            ada_sums(l, 2 * c - 1)
                    release(ng, tiles_dve)
                    release(nu, tiles_dve)
                    for i in range(2):
                        made_so_far[0] += conditions(l, 2 * c + i)
                        released[state["chunk"]] = (S["ada_made"], made_so_far[0])
                        state["chunk"] += 1
                for c in range(2):
                    if c:
                        ada_sums(l, 10)
                        ada_sums(l, 11)
                    for b in range(4):
                        open_bank(b)
                    for k0 in range(0, FT, KT):
                        n, w = next_chunk()
                        nk = w.shape[1]
                        for m in range(4):
                            for k in range(k0, k0 + nk):
                                if c == 0 and m == 0:
                                    turn.take(S["hidden"])
                                last = mm(ps[:, m, 0:T], w[:, k - k0, m * P:(m + 1) * P], ff[:, k, :],
                                          start=(k == 0), stop=(k == FT - 1))
                            if k0 + nk == FT:
                                close_bank(m, last, tiles_act, S["proj_copied"])
                        if k0 + nk < FT:
                            turn.give(last, down_part)
                        release(n, down_part if k0 + nk < FT else tiles_act)
                state["bank"] = 3
                stats()

            ffn(0)

            stats()
            dense(h, tiles_act, S["mq"], S["h_ready"])
            dense(h, tiles_act, S["mk"])
            b = stat_bank()
            for t in range(TT):
                for k in range(KT):
                    mm(ps[:, b, 16 * t:16 * t + 16], h[:, k, t * P:(t + 1) * P], gw[:, k, :],
                       start=(k == 0), stop=False)
                last = mm(ps[:, b, 16 * t:16 * t + 16], ones_row, rowv("gate_b"), start=False, stop=True)
            close_bank(b, last, tiles_dve, S["gates_tok"])
            for c in range(2):
                dense(h, tiles_act, S["mo"])
            turn.take(S["gates_tok"])
            b = stat_bank()
            for g in range(2):
                for t in range(TT):
                    last = nc.tensor.transpose(ps[0:8, b, (2 * g + t) * P:(2 * g + t + 1) * P],
                                               gtok[:, t, 8 * g:8 * g + 8], ident)
            close_bank(b, last, tiles_dve, S["gates_head"])
            for c in range(2):
                n, w = next_chunk()
                for t in range(TT):
                    b = next_bank()
                    for k in range(KT):
                        mm(ps[:, b, :], h[:, k, t * P:(t + 1) * P], w[:, k, :], start=(k == 0), stop=False)
                    last = mm(ps[:, b, :], ones_row, rowv("v_b")[:, c * CH:(c + 1) * CH], start=False, stop=True)
                    close_bank(b, last, tiles_act, S["mv"])
                release(n, tiles_act)
            turn.take(S["gate_a"])
            b = stat_bank()
            for t in range(TT):
                last = nc.tensor.transpose(ps[:, b, 8 * t:8 * t + 8], ghead[:, 0, t * P:(t + 1) * P],
                                           ident[0:8, 0:8])
            close_bank(b, last, tiles_dve, S["acol_ready"])

            def head_scores(n):
                b = next_bank()
                close_bank(b, mm(ps[:, b, 0:T], sel8[:, n, :], ghead[:, 2, :], start=True, stop=True),
                           tiles_dve, S["exponents"])
                b = next_bank()
                lo = 64 * (n % 2)
                kk, qq = k_m[lo:lo + 64, n // 2, :], q_m[lo:lo + 64, n // 2, :]
                mm(ps[:, b, 0:T], kk[:, 0:P], qq, start=True, stop=True)
                close_bank(b, mm(ps[:, b, T:T + P], kk[:, P:T], qq[:, P:T], start=True, stop=True),
                           tiles_dve, S["weighted"])

            turn.take(S["gate_expm"])
            turn.take(S["mq"], 4)
            turn.take(S["mk"], 4)
            turn.take(S["mv"], 4)
            head_scores(0)
            head_scores(1)
            for n in range(HEADS):
                turn.take(S["weighted"])
                if n + 2 < HEADS:
                    head_scores(n + 2)
                open_bank(7)
                mm(ps[:, 7, T:2 * T], sel8[:, n, :], ghead[:, 3, :], start=True, stop=True)
                mm(ps[:, 7, 0:T], ones[:], pm[:, n % 2, 0:T], start=True, stop=False, skip_group_check=True)
                close_bank(7, mm(ps[:, 7, P:T], ones[:], pm[:, n % 2, T:T + P], start=False, stop=True,
                                 skip_group_check=True), tiles_act, S["den_read"])
                open_bank(6)
                mm(ps[:, 6, 0:T], v_m[:, 0, n * P:(n + 1) * P], pm[:, n % 2, 0:T], start=True, stop=False,
                   skip_group_check=True)
                close_bank(6, mm(ps[:, 6, P:T], v_m[:, 1, n * P:(n + 1) * P], pm[:, n % 2, T:T + P],
                                 start=False, stop=True, skip_group_check=True), tiles_dve, S["head_out"])
            for n in range(HEADS):
                turn.take(S["squares"])
                b = stat_bank()
                close_bank(b, mm(ps[:, b, 0:T], ones[:], sq[:, n, :], start=True, stop=True),
                           tiles_act, S["head_roots"])
            project_norm(y_m, KT)
            ffn(1)

            stats()
            stats()
            n, w = next_chunk()
            product(w, 0, hc, tiles_act, S["kraw_ready"], S["hc_ready"])
            product(w, 0, h, tiles_act, S["kraw_ready"], S["h_ready"])
            b = next_bank()
            for t in range(4):
                src = hc if t < 2 else h
                for k in range(KT):
                    last = mm(ps[:, b, t * P:(t + 1) * P], src[:, k, (t % 2) * P:(t % 2 + 1) * P],
                              w[:, k, P:2 * P], start=(k == 0), stop=(k == KT - 1))
            close_bank(b, last, tiles_act, S["vals"])
            release(n, tiles_act)
            dense(h, tiles_act, S["qraw_ready"])
            dense(h, tiles_act, S["u_gelu"])
            n, w = next_chunk()
            for t in range(TT):
                b = next_bank()
                for k in range(KT):
                    last = mm(ps[:, b, :], h[:, k, t * P:(t + 1) * P], w[:, k, :], start=(k == 0), stop=(k == KT - 1))
                close_bank(b, last, tiles_act, S["z_gelu"])
            release(n, tiles_act)
            turn.take(S["kraw_ready"], 2)
            for kv in range(2):
                b = next_bank()
                close_bank(b, mm(ps[:, b, 0:T], perm[:, 1 + kv, :], kraw[:, 0, :], start=True, stop=True),
                           tiles_act, S["k_ctx"])
                b = next_bank()
                mm(ps[:, b, 0:T], perm[:, 1 + kv, :], kraw[:, 1, :], start=True, stop=True)
                close_bank(b, mm(ps[:, b, T:2 * T], perm[:, 3 + kv, :], kraw[:, 1, :], start=True, stop=True),
                           tiles_dve, S["k_rope_read"])
            turn.take(S["qraw_ready"], 4)
            for j in range(HTL):
                b = next_bank()
                close_bank(b, mm(ps[:, b, 0:T], perm[:, 0, :], q_a[:, j, :], start=True, stop=True),
                           tiles_dve, S["q_rope_read"])

            def att_scores(i):
                n, t = i // 2, i % 2
                lo = 64 * (n % 2)
                b = next_bank()
                close_bank(b, mm(ps[:, b, :], q_a[lo:lo + 64, n // 2, t * P:(t + 1) * P], kd[lo:lo + 64, n // 4, :],
                                 start=True, stop=True), tiles_dve, S["scores_read"])

            turn.take(S["k_ctx"], 2)
            turn.take(S["vals"])
            turn.take(S["rotated"])

            def att_turn(i):
                turn.take(S["probs"])
                b = stat_bank()
                for k in range(4):
                    last = nc.tensor.transpose(ps[:, b, k * P:(k + 1) * P], pexp[:, i % 2, k * P:(k + 1) * P], ident)
                close_bank(b, last, tiles_act, S["pt_ready"])

            for i in range(3):
                att_scores(i)
            att_turn(0)
            for i in range(2 * HEADS):
                if i + 3 < 2 * HEADS:
                    att_scores(i + 3)
                if i + 1 < 2 * HEADS:
                    att_turn(i + 1)
                n, t = i // 2, i % 2
                turn.take(S["pt_ready"])
                b = 6 + (n // 2) % 2
                if i % 4 == 0:
                    open_bank(b)
                lo = 64 * (n % 2)
                for k in range(4):
                    last = mm(ps[lo:lo + 64, b, t * P:(t + 1) * P], v_a[:, k, 64 * (n // 4):64 * (n // 4) + 64],
                              pt[:, i % 2, k * P:(k + 1) * P], start=(k == 0), stop=(k == 3))
                if i % 4 == 3:
                    close_bank(b, last, tiles_act, S["att_out"])
            turn.take(S["z_normed"])
            for j in range(HTL):
                b = next_bank()
                for t in range(TT):
                    mm(ps[:, b, t * P:(t + 1) * P], selb[:, j, :], bsp[:], start=True, stop=False,
                       skip_group_check=True)
                    for i in range(2):
                        last = mm(ps[64 * i:64 * i + 64, b, t * P:(t + 1) * P],
                                  z_a[:, t, (2 * j + i) * 64:(2 * j + i + 1) * 64], wsp[:, 2 * j + i, :],
                                  start=False, stop=True, skip_group_check=True)
                close_bank(b, last, tiles_dve, S["mixed"])

            def latent_project(src):
                dense(src, tiles_dve, S["x_added"])
                dense(src, tiles_dve, S["x_added"])
                stats()

            turn.take(S["att_out"], 4)
            turn.take(S["mixed"], 4)
            latent_project(mix)

            def experts(l):
                e_ = E[l]
                b = stat_bank()
                for t in range(TT):
                    for k in range(KT):
                        if t == 0:
                            turn.take(S["h_ready"])
                        mm(ps[:, b, NLOG * t:NLOG * (t + 1)], h[:, k, t * P:(t + 1) * P], rw[:, l, k, :],
                           start=(k == 0), stop=False)
                    last = mm(ps[:, b, NLOG * t:NLOG * (t + 1)], ones_row,
                              rowv("router_b")[:, NLOG * l:NLOG * (l + 1)], start=False, stop=True)
                close_bank(b, last, tiles_dve, S["logits_read"])
                for t in range(TT):
                    for c in range(2):
                        b = next_bank()
                        for k in range(4):
                            last = nc.tensor.transpose(ps[:, b, k * P:(k + 1) * P],
                                                       h[:, 4 * c + k, t * P:(t + 1) * P], ident)
                        close_bank(b, last, tiles_act, S["htok_ready"])
                turn.take(S["chosen_ready"])
                b = next_bank()
                one, two = chosen[:, 0, 0:NEXP], chosen[:, 1, 0:NEXP]
                mm(ps[:, b, 0:NEXP], below, one, start=True, stop=True)
                mm(ps[:, b, NEXP:2 * NEXP], ones[:], one, start=True, stop=False)
                mm(ps[:, b, NEXP:2 * NEXP], below, two, start=False, stop=True)
                mm(ps[:, b, 2 * NEXP:3 * NEXP], ones[:], one, start=True, stop=False)
                close_bank(b, mm(ps[:, b, 2 * NEXP:3 * NEXP], ones[:], two, start=False, stop=True),
                           tiles_dve, S["crowd_ready"])
                turn.take(S["crowd_ready"])
                turn.take(S["htok_ready"], 4)
                most = pe.value_load(crowd[0:1, 0:1])
                for b in range(8):
                    open_bank(b)
                    owner[b] = None
                for b in range(4, 8):
                    mm(ps[:, b, :], zeros[:, 0:P], con[:, 0:512], start=True, stop=False, skip_group_check=True)
                first = moe_first[l]
                assert first == state["chunk"]
                with pe.If(most > CAP):
                    all_tokens(e_, first)
                with pe.Else():
                    gathered_tokens(e_, first)
                state["chunk"] += 3 * NEXP
                for b in range(4, 8):
                    close_bank(b, mm(ps[:, b, :], zeros[:, 0:P], con[:, 0:512], start=False, stop=True,
                                     skip_group_check=True), tiles_dve, S["x_added"], reads=2)
                stats()

            def matrices(first, e):
                n = [first + 2 * e, first + 2 * e + 1, first + 4 + e]
                slots = [j % RING for j in n]
                return slots, [16 * (j // RING + 1) for j in n], [
                    ring[:, slots[j], :].rearrange("p (k c) -> p k c", k=KT if j < 2 else HTL) for j in range(3)]

            def all_tokens(e_, first):
                with pe.Fori(0, NEXP // 2) as i:
                    for e in range(2):
                        slots, loads, (wg, wu, wd) = matrices(first, e)
                        pe.wait_ge(e_["diag"], 2 * i + e + 1)
                        pe.wait_ge(e_["row_copied"], 2 * i + e + 1)
                        mm(ps[:, 3, 0:P], ones[:], dg[:, e, 0:P], start=True, stop=True)
                        mm(ps[:, 3, P:T], ones[:], dg[:, e, P:T], start=True, stop=True).then_inc(e_["row_full"], 1)
                        pe.wait_ge(slot_loaded[slots[0]], 16 * i + loads[0])
                        pe.wait_ge(slot_loaded[slots[1]], 16 * i + loads[1])
                        for m in range(HTL):
                            pe.wait_ge(e_["gate_freed"], 8 * i + 4 * e + m + 1)
                            for k in range(KT):
                                last = mm(ps[:, 2 * (m % 2), 0:T], wg[:, k, m * P:(m + 1) * P], h[:, k, :],
                                          start=(k == 0), stop=(k == KT - 1))
                            last.then_inc(e_["gate_full"], 1)
                            pe.wait_ge(e_["up_freed"], 8 * i + 4 * e + m + 1)
                            for k in range(KT):
                                last = mm(ps[:, 1, 0:T], wu[:, k, m * P:(m + 1) * P], h[:, k, :],
                                          start=(k == 0), stop=(k == KT - 1))
                            last.then_inc(e_["up_full"], 1)
                        pe.wait_ge(slot_loaded[slots[2]], 16 * i + loads[2])
                        for k in range(HTL):
                            pe.wait_ge(e_["hid_ready"], 8 * i + 4 * e + k + 1)
                            for m in range(KT):
                                last = mm(ps[:, 4 + m // 2, (m % 2) * T:(m % 2 + 1) * T],
                                          wd[:, k, m * P:(m + 1) * P], hid[:, e, k * T:(k + 1) * T],
                                          start=False, stop=False, skip_group_check=True)
                        last.then_inc(e_["down_done"], 1)
                pe.wait_ge(e_["row_copied"], NEXP + 1)

            def gather(e_, pair):
                pe.wait_ge(e_["masks_ready"], pair + 1)
                for b in range(2):
                    for k in range(4):
                        for t in range(TT):
                            last = mm(ps[:, 2 + b, k * PAIR:(k + 1) * PAIR],
                                      htok[:, t, (4 * b + k) * P:(4 * b + k + 1) * P], pick[:, t, :],
                                      start=(t == 0), stop=(t == TT - 1))
                    last.then_inc(e_["gathered"], 1)

            def gathered_tokens(e_, first):
                gather(e_, 0)
                with pe.Fori(0, NEXP // 2) as i:
                    pe.wait_ge(e_["xg_ready"], 2 * i + 2)
                    for e in range(2):
                        slots, loads, (wg, wu, _) = matrices(first, e)
                        for j, w in enumerate((wg, wu)):
                            pe.wait_ge(slot_loaded[slots[j]], 16 * i + loads[j])
                            for k in range(KT):
                                last = mm(ps[e * CAP:(e + 1) * CAP, j, :], xg[:, k, e * CAP:(e + 1) * CAP],
                                          w[:, k, :], start=(k == 0), stop=(k == KT - 1))
                            last.then_inc(e_["gate_full"], 1)
                        if e == 0:
                            for t in range(TT):
                                last = nc.tensor.transpose(ps[:, 2, t * P:(t + 1) * P], weigh[:, t, :], ident)
                            last.then_inc(e_["weights_turned"], 1)
                    pe.wait_ge(e_["spread_ready"], i + 1)
                    gather(e_, i + 1)
                    pe.wait_ge(e_["hid_ready"], i + 1)
                    for m in range(HTL):
                        last = nc.tensor.transpose(ps[:, 0, m * P:(m + 1) * P], hs[:, m * P:(m + 1) * P], ident)
                    last.then_inc(e_["hid_turned"], 1)
                    pe.wait_ge(e_["hg_ready"], i + 1)
                    for e in range(2):
                        slots, loads, (_, _, wd) = matrices(first, e)
                        pe.wait_ge(slot_loaded[slots[2]], 16 * i + loads[2])
                        for c in range(2):
                            for k in range(HTL):
                                at = k * PAIR + e * CAP
                                last = mm(ps[e * CAP:(e + 1) * CAP, c, :], hg[:, at:at + CAP],
                                          wd[:, k, c * 512:(c + 1) * 512], start=(k == 0), stop=(k == HTL - 1))
                            if e == 1 and c == 0:
                                last.then_inc(e_["half_done"], 1)
                        last.then_inc(e_["down_done"], 1)
                    for m in range(KT):
                        if m % 4 == 0:
                            pe.wait_ge(e_["yt_ready"], 2 * i + m // 4 + 1)
                        mm(ps[:, 4 + m // 2, (m % 2) * T:(m % 2 + 1) * T], yt[:, m * P:(m + 1) * P], spread,
                           start=False, stop=False, skip_group_check=True)
                pe.wait_ge(e_["xg_ready"], NEXP + 2)

            experts(0)

            ready = S["h_ready"]
            for free, full in (("cgate", tiles_act), ("cvalue", tiles_dve)) * 2 + (("bgate", tiles_act),) * 2:
                dense(h, full, S[free], ready)
                ready = None
            for k in range(KT):
                turn.take(S["mixed"])
            latent_project(cvo)
            experts(1)

        @block.sync
        def _(sp):
            for dst, src in ((vec[:], a["vec"]), (con[:], a["con"]), (misc[32:33, :], a["row"]), (misc[0:8, 0:SELS], a["sel"]), (gw[:], a["gate_w"]),
                             (rw[:], a["router_w"]), (wsp[:], a["w_sp"]), (bsp[:], a["b_sp"])):
                sp.dma_start(dst, src).then_inc(consts_loaded, 16)

            def load(n):
                if n >= RING:
                    sp.wait_ge(*released[n - RING])
                put(n)

            def put(n):
                src, nk, cols = chunks[n]
                sp.dma_start(ring[:, n % RING, 0:nk * cols].rearrange("p (k c) -> p k c", k=nk), src).then_inc(
                    slot_loaded[n % RING], 16)

            def load_experts(l):
                first, e_ = moe_first[l], E[l]
                weights = [a["w_gate"], a["w_up"], a["w_down"]]
                order = [(0, 0), (1, 0), (0, 1), (1, 1), (2, 0), (2, 1)]
                for j, (w, e) in enumerate(order):
                    n = first + j
                    sp.wait_ge(*released[n - RING])
                    sp.dma_start(ring[:, n % RING, :], weights[w][l, e]).then_inc(slot_loaded[n % RING], 16)
                sp.wait_ge(S["crowd_ready"], l + 1)
                most = sp.value_load(crowd[0:1, 0:1])

                def rest(done):
                    with sp.Fori(0, NEXP // 2 - 1) as i:
                        for j, (w, e) in enumerate(order):
                            s_, per, at = done(w, e)
                            sp.wait_ge(s_, per * i + at)
                            slot = (first + j) % RING
                            sp.dma_start(ring[:, slot, :], weights[w][l, 2 * i + (2 + e)]).then_inc(
                                slot_loaded[slot], 16)
                    for j, (w, e) in enumerate(order):
                        n = first + 3 * NEXP + j
                        if n < len(chunks):
                            s_, per, at = done(w, e)
                            sp.wait_ge(s_, per * (NEXP // 2 - 1) + at)
                            put(n)

                with sp.If(most > CAP):
                    rest(lambda w, e: ((e_["gate_full"], 8, 4 * e + 4), (e_["up_full"], 8, 4 * e + 4),
                                       (e_["down_done"], 2, e + 1))[w])
                with sp.Else():
                    rest(lambda w, e: (e_["down_done"], 2, e + 1) if w == 2 else (e_["gate_full"], 4, 2 * e + w + 1))

            for n in range(moe_first[0]):
                load(n)
            load_experts(0)
            for n in range(moe_first[0] + 3 * NEXP + RING, moe_first[1]):
                load(n)
            load_experts(1)

        @block.gpsimd
        def _(pool):
            for dst, value in ((ones[:], 1.0), (bd[:], 0.0), (cpad[:, :, 0:CK - 1], 0.0), (rpad[:, :, 0:LK - 1], 0.0),
                               (eps[:], EPS), (zeros[:], 0.0)):
                nc.gpsimd.memset(dst, value).then_inc(memsets, 1)

        @block.scalar
        def _(act):
            turn = Turns(act)
            where = iter(bank_of[tiles_act])

            def A(out_, in_, f, bias=0.0, scale=1.0, **kw):
                return nc.scalar.activation(out_, in_, f, bias=bias, scale=scale, **kw)

            def tile():
                turn.take(tiles_act)
                return ps[:, next(where), :]

            def squares(src, ready=None, n=KT):
                for k in range(n):
                    if ready is not None:
                        turn.take(ready)
                    turn.give(A(sq[:, k, :], src[:, k, :], ACT.Square), S["squares"])

            def norm_root(count, to=root):
                turn.give(A(to[:], tile()[:, 0:T], ACT.Sqrt, bias=eps[:], scale=1.0 / count), S["roots"])

            def ada_out(l, c):
                for w in range(conditions(l, c)):
                    turn.give(A(ada[:, l, 4 * c:4 * c + 4, w], tile()[:, 0:8].rearrange("p (a b) -> p a b", b=2)[:, :, 0],
                                ACT.Copy), S["ada_raw"])

            act.dma_start(x[:], a["x"]).then_inc(x_loaded, 16)
            act.wait_ge(memsets, 6)
            for g in range(2):
                for half in range(2):
                    act.dma_start(bd[64 * half:64 * half + 64, g, :, 64 * half:64 * half + 64],
                                  a["lru_w"][g, half]).then_inc(blocks_loaded, 16)
            act.wait_ge(consts_loaded, 16 * 8)
            turn.give(A(silu_c[:], v("c").rearrange("p (a b) -> p a b", b=2), ACT.Sigmoid), S["c_sigmoid"])
            turn.give(A(sgu_g[:], tile()[:, 0:HALF], ACT.Copy), S["rows_spread"])
            turn.give(A(sink[:], tile()[:, 0:8], ACT.Copy), S["rows_spread"])

            act.wait_ge(x_loaded, 16)
            squares(x)
            norm_root(D)
            b_in = v("ab_b_in")
            for j in range(HTL):
                turn.give(A(sgate[:, j, :], tile()[:, 0:T], ACT.Sigmoid, bias=b_in[:, 4 + j:5 + j]), S["glu_gate"])
            for j in range(HTL):
                turn.give(A(rpad[:, j, LK - 1:], tile()[:, 0:T], ACT.Identity, bias=b_in[:, 12 + j:13 + j]),
                          S["rec_in"])
            for j in range(HTL):
                turn.give(A(gin[:, j, :], tile()[:, 0:T], ACT.Gelu_apprx_tanh, bias=b_in[:, 8 + j:9 + j]),
                          S["gelu_in"])
            for j in range(HTL):
                turn.give(A(th[:, j, :], tile()[:, 0:T], ACT.Sigmoid, bias=v("b_a")[:, j:j + 1]), S["lru_gate"])
                turn.give(A(bx[:, j, :], tile()[:, 0:T], ACT.Sigmoid, bias=v("b_x")[:, j:j + 1]), S["lru_gate"])
            turn.take(S["lam_abs"])
            turn.give(A(lamt[:, 4:8], lamt[:, 0:4], ACT.Exp, scale=-1.0), achain)
            turn.own(achain)
            turn.give(A(lamt[:, 8:12], lamt[:, 4:8], ACT.Ln, bias=1.0), S["lam_ln"])
            turn.take(S["lam_rate"])
            turn.own(S["lru_gate"])
            for j in range(HTL):
                last = A(th[:, j, :], th[:, j, :], ACT.Tanh, scale=lamt[:, 16 + j:17 + j])
                turn.give(last, S["lru_tanh"])
            turn.own(S["lru_tanh"])
            turn.give(A(den_a[:], th[:], ACT.Sqrt), S["lru_root"])
            for n in range(PE_CONV * CK):
                if n % (TAPS // 2) == 0 and n >= TAPS:
                    turn.take(S["taps_used"])
                col = (HTL - PE_CONV) * CK + n
                turn.give(A(taps[:, n % TAPS, :], ident, ACT.Identity, scale=v("conf_w")[:, col:col + 1]),
                          S["tap_ready"])
            for j in range(HTL - PE_CONV, HTL):
                turn.give(A(cv[:, j, :], tile()[:, 0:T], ACT.Identity, bias=v("conf_b")[:, j:j + 1]),
                          S["tiles_convolved"])
            squares(cv, S["ln_centred"], HTL)
            norm_root(HALF)
            for j in range(HTL):
                turn.take(S["ln_normed"])
                turn.give(A(sgate[:, j, :], cv[:, j, :], ACT.Sigmoid), S["ln_sigmoid"])

            def project_norm(l=None):
                for m in range(KT):
                    if m == KT // 2 and l is not None:
                        ada_out(l, 10)
                        ada_out(l, 11)
                    turn.give(A(h[:, m, :], tile()[:, 0:T], ACT.Copy), S["proj_copied"])
                    turn.own(S["proj_copied"])
                    turn.give(A(sq[:, m, :], h[:, m, :], ACT.Square), S["squares"])
                norm_root(D)

            def ffn(l):
                squares(x, S["x_ready"])
                norm_root(D)
                for m in range(FT):
                    turn.give(A(sgt[:, m % 2, :], tile()[:, 0:T], ACT.Sigmoid), S["ffn_sig"])
                    if m % 4 == 0 and m:
                        ada_out(l, 2 * (m // 4) - 2)
                        ada_out(l, 2 * (m // 4) - 1)
                project_norm(l)

            project_norm()
            ffn(0)

            squares(x, S["x_ready"])
            norm_root(D)
            mb = v("ml_b")
            for j in range(HTL):
                turn.give(A(q_m[:, j, :], tile()[:, 0:T], ACT.Identity, bias=mb[:, j:j + 1]), S["mq"])
            turn.take(S["kb_scaled"])
            for j in range(HTL):
                turn.give(A(k_m[:, j, :], tile()[:, 0:T], ACT.Identity, bias=lamt[:, 20 + j:21 + j], scale=0.125),
                          S["mk"])
            for j in range(KT):
                turn.give(A(so[:, j, :], tile()[:, 0:T], ACT.Sigmoid, bias=mb[:, 8 + j:9 + j]), S["mo"])
            turn.take(S["f_abs"])
            turn.give(A(ghead[:, 2, :], ghead[:, 2, :], ACT.Exp, scale=-1.0), achain)
            turn.own(achain)
            turn.give(A(ghead[:, 2, :], ghead[:, 2, :], ACT.Ln, bias=1.0), S["f_ln"])
            for c in range(2):
                for t in range(TT):
                    turn.give(A(v_m[:, t, c * CH:(c + 1) * CH], tile(), ACT.Copy), S["mv"])
            turn.take(S["gate_m"])
            turn.give(A(ghead[:, 3, :], ghead[:, 3, :], ACT.Exp, scale=-1.0), S["gate_expm"])

            def decay(n):
                turn.take(S["exponents"])
                turn.give(A(dexp[:, n % 2, :], darg[:, n % 2, :], ACT.Exp, scale=-1.0), S["decays"])

            decay(0)
            decay(1)
            for n in range(HEADS):
                if n + 2 < HEADS:
                    decay(n + 2)
                turn.give(A(absd[:, n % 2, :], tile()[:, 0:T], ACT.Abs), S["absden"])
            squares(y_m, S["head_out"])
            for n in range(HEADS):
                turn.give(A(sq[:, n, :], tile()[:, 0:T], ACT.Sqrt, bias=eps[:], scale=1.0 / P), S["head_roots"])
            project_norm()
            ffn(1)

            turn.own(S["roots"])
            act.dma_start(ctxr[:], a["ctx"]).then_inc(ctx_loaded, 16)
            act.wait_ge(ctx_loaded, 16)
            squares(ctxr)
            norm_root(D, root_c)
            squares(x, S["x_ready"])
            norm_root(D)
            for s in range(2):
                turn.give(A(kraw[:, s, :], tile()[:, 0:T], ACT.Copy), S["kraw_ready"])
            turn.give(A(v_a[:], tile().rearrange("p (a b) -> p a b", a=4), ACT.Copy), S["vals"])
            for j in range(HTL):
                turn.give(A(q_a[:, j, :], tile()[:, 0:T], ACT.Copy), S["qraw_ready"])
            for j in range(HTL):
                turn.give(A(u_a[:, j, :], tile()[:, 0:T], ACT.Gelu), S["u_gelu"])
            for t in range(TT):
                turn.give(A(z_a[:, t, :], tile(), ACT.Gelu), S["z_gelu"])
            for kv in range(2):
                turn.give(A(kd[:, kv, 0:T], tile()[:, 0:T], ACT.Copy), S["k_ctx"])
            turn.take(S["z_centred"])
            for t in range(TT):
                turn.give(A(z_a[:, t, :], zc[:, t, :], ACT.Square, accum_out=small[:, 4 + t:5 + t]), S["z_sq"])
            turn.own(S["z_sq"])
            turn.give(A(small[:, 6:8], small[:, 4:6], ACT.Sqrt, bias=eps[:], scale=1.0 / HALF), S["z_root"])

            def att_exp(i):
                turn.take(S["maxima"])
                turn.give(A(pexp[:, i % 2, :], sm[:, i % 2, :], ACT.Exp, bias=small[:, 10 + i % 2:11 + i % 2],
                            accum_out=small[:, 12 + i % 2:13 + i % 2]), achain)
                turn.own(achain)
                turn.give(A(small[:, 14 + i % 2:15 + i % 2], sink[:, i // 2:i // 2 + 1], ACT.Exp,
                            bias=small[:, 10 + i % 2:11 + i % 2]), S["exps"])

            def att_turned(i):
                turn.give(A(pt[:, i % 2, :], tile(), ACT.Copy), S["pt_ready"])

            att_exp(0)
            att_exp(1)
            att_turned(0)
            for i in range(2 * HEADS):
                if i + 2 < 2 * HEADS:
                    att_exp(i + 2)
                if i + 1 < 2 * HEADS:
                    att_turned(i + 1)
                if i % 4 == 3:
                    turn.give(A(mix[:, i // 4, :], tile()[:, 0:T], ACT.Copy), S["att_out"])

            def latent_norm():
                squares(x, S["x_added"])
                norm_root(D)

            latent_norm()

            def experts(l):
                e_ = E[l]
                for t in range(TT):
                    turn.take(S["router_max"])
                    turn.give(A(rt[:, 5, 0:4], lg[:, t, 0:4], ACT.Exp, bias=small[:, 20:21],
                                accum_out=small[:, 21:22]), S["router_exp"])
                    turn.take(S["router_gap"])
                    turn.give(A(small[:, 23:24], small[:, 22:23], ACT.Exp), S["router_gexp"])
                for t in range(TT):
                    for c in range(2):
                        turn.give(A(htok[:, t, c * 512:(c + 1) * 512], tile(), ACT.Copy), S["htok_ready"])
                turn.take(S["crowd_ready"])
                most = act.value_load(crowd[0:1, 0:1])
                with act.If(most > CAP):
                    with act.Fori(0, NEXP // 2) as i:
                        for e in range(2):
                            act.wait_ge(e_["row_full"], 2 * i + e + 1)
                            A(gb[:, e, :], ps[:, 3, 0:T], ACT.Copy).then_inc(e_["row_copied"], 1)
                            for m in range(HTL):
                                act.wait_ge(e_["gate_full"], 8 * i + 4 * e + m + 1)
                                A(esg[:, m % 2, :], ps[:, 2 * (m % 2), 0:T], ACT.Sigmoid).then_inc(e_["gate_sig"], 1)
                with act.Else():
                    def slots_in(pair):
                        for b in range(2):
                            act.wait_ge(e_["gathered"], 2 * pair + b + 1)
                            A(xg[:, 4 * b:4 * b + 4, :], ps[:, 2 + b, :].rearrange("p (a b) -> p a b", a=4),
                              ACT.Copy).then_inc(e_["xg_ready"], 1)

                    slots_in(0)
                    with act.Fori(0, NEXP // 2) as i:
                        act.wait_ge(e_["gate_full"], 4 * i + 3)
                        A(sg, ps[:, 0, :], ACT.Sigmoid).then_inc(e_["gate_sig"], 1)
                        slots_in(i + 1)
                        act.wait_ge(e_["half_done"], i + 1)
                        A(yt[:, 0:512], ps[:, 0, :], ACT.Copy).then_inc(e_["yt_ready"], 1)
                        act.wait_ge(e_["down_done"], 2 * i + 2)
                        A(yt[:, 512:D], ps[:, 1, :], ACT.Copy).then_inc(e_["yt_ready"], 1)
                latent_norm()

            experts(0)
            for c in range(6):
                if c in (0, 2):
                    for j in range(HTL):
                        turn.give(A(cg[:, 2 * c + j, :], tile()[:, 0:T], ACT.Copy), S["cgate"])
                elif c >= 4:
                    for j in range(HTL):
                        turn.give(A(bg[:, 4 * (c - 4) + j, :], tile()[:, 0:T], ACT.Copy), S["bgate"])
            latent_norm()
            experts(1)

        @block.vector
        def _(dve):
            turn = Turns(dve)
            where = iter(bank_of[tiles_dve])
            gates = iter(gate_bank)
            V = nc.vector

            def step(instruction, signal=vchain):
                turn.give(instruction, signal)
                turn.own(signal)

            def tile():
                turn.take(tiles_dve)
                return ps[:, next(where), :]

            def stt(out_, in0, scalar, in1, op0, op1):
                return V.scalar_tensor_tensor(out=out_, in0=in0, scalar=scalar, in1=in1, op0=op0, op1=op1)

            def inverse_root(src=root):
                turn.take(S["roots"])
                step(V.reciprocal(rstd[:], src[:]))

            def pre_norm(g):
                inverse_root()
                for k in range(KT):
                    turn.give(stt(h[:, k, :], x[:, k, :], g[:, k:k + 1], rstd[:], ALU.mult, ALU.mult), S["h_ready"])

            def post_norm(g):
                inverse_root()
                for k in range(KT + 1):
                    if k < KT:
                        turn.give(stt(h[:, k, :], h[:, k, :], g[:, k:k + 1], rstd[:], ALU.mult, ALU.mult), vchain)
                    if k:
                        turn.own(vchain, k < KT)
                        turn.give(V.tensor_tensor(x[:, k - 1, :], x[:, k - 1, :], h[:, k - 1, :], ALU.add),
                                  S["x_ready"])
                turn.own(S["x_ready"])

            def gain(name, l):
                return v(name)[:, 8 * l:8 * l + 8]

            dve.wait_ge(memsets, 6)
            dve.wait_ge(consts_loaded, 16 * 8)
            step(stt(lamt[:, 0:4], v("lam"), -1.0, v("lam"), ALU.mult, ALU.max), S["lam_abs"])
            step(V.tensor_scalar(lamt[:, 20:24], v("ml_b")[:, 4:8], 0.125, None, ALU.mult), S["kb_scaled"])
            turn.take(S["c_sigmoid"])
            step(V.tensor_tensor(silu_c[:], silu_c[:], v("c").rearrange("p (a b) -> p a b", b=2), ALU.mult),
                 S["silu_c"])

            dve.wait_ge(x_loaded, 16)
            pre_norm(gain("pre_mix_g", 0))
            b_in = v("ab_b_in")
            for j in range(HTL):
                turn.take(S["glu_gate"])
                step(stt(cpad[:, j, CK - 1:], tile()[:, 0:T], b_in[:, j:j + 1], sgate[:, j, :], ALU.add, ALU.mult),
                     S["glu"])

            def conv(dst, src, w, bias, taps, done, tiles=HTL):
                for k in range(taps):
                    for j in range(tiles):
                        s, wk = src[:, j, k:k + T], w[:, j * taps + k:j * taps + k + 1]
                        if k == 0:
                            turn.give(V.tensor_scalar(dst[:, j, :], s, wk, bias[:, j:j + 1], ALU.mult, ALU.add), vchain)
                            continue
                        turn.own(vchain, tiles - 1)
                        last = stt(dst[:, j, :], s, wk, dst[:, j, :], ALU.mult, ALU.add)
                        turn.give(last, vchain)
                turn.own(vchain)
                for j in range(tiles):
                    turn.give(V.tensor_copy(small[:, 40 + j:41 + j], dst[:, j, 0:1]), done)

            turn.take(S["rec_in"], HTL)
            conv(xr, rpad, v("lru_w"), v("lru_b"), LK, S["lru_conv"])
            turn.take(S["lam_ln"])
            step(stt(lamt[:, 12:16], v("lam"), -1.0, zeros[:, 0:4], ALU.mult, ALU.max))
            step(V.tensor_tensor(lamt[:, 12:16], lamt[:, 12:16], lamt[:, 8:12], ALU.add))
            step(V.tensor_scalar(lamt[:, 16:20], lamt[:, 12:16], LRU_C / 2, None, ALU.mult), S["lam_rate"])
            conv(cv, cpad, v("conf_w"), v("conf_b"), CK, S["conf_conv"], HTL - PE_CONV)
            turn.take(S["lru_gate"], 2 * HTL)
            turn.take(S["lru_tanh"], HTL)
            u = ymix[:, HTL:KT, :]
            step(V.tensor_tensor(bx[:], bx[:], xr[:], ALU.mult))
            step(V.tensor_scalar(u, th[:], 1.0, None, ALU.add))
            step(V.reciprocal(u, u))
            turn.take(S["lru_root"])
            step(V.tensor_tensor(den_a[:], den_a[:], u, ALU.mult))
            step(stt(bx[:], bx[:], 2.0, den_a[:], ALU.mult, ALU.mult))
            step(V.tensor_scalar(th[:], u, 2.0, -1.0, ALU.mult, ALU.add))
            for j in range(HTL):
                turn.give(V.tensor_tensor_scan(den_a[:, j, :], th[:, j, :], bx[:, j, :], 0.0, ALU.mult, ALU.add),
                          vchain)
            turn.own(vchain)
            turn.take(S["gelu_in"], HTL)
            step(V.tensor_tensor(ymix[:, HTL:KT, :], den_a[:], gin[:], ALU.mult))
            step(V.tensor_scalar(tmp[:, 0, :], tile()[:, 0:T], 1.0 / HALF, None, ALU.mult), S["ln_mean"])
            turn.take(S["tiles_convolved"], PE_CONV)
            for j in range(HTL):
                step(V.tensor_tensor(cv[:, j, :], cv[:, j, :], tmp[:, 0, :], ALU.subtract), S["ln_centred"])
            inverse_root()
            for j in range(HTL):
                step(stt(cv[:, j, :], cv[:, j, :], v("ln_g")[:, j:j + 1], rstd[:], ALU.mult, ALU.mult))
                step(V.tensor_scalar(cv[:, j, :], cv[:, j, :], v("ln_b")[:, j:j + 1], None, ALU.add), S["ln_normed"])
            for j in range(HTL):
                turn.take(S["ln_sigmoid"])
                step(V.tensor_tensor(ymix[:, j, :], cv[:, j, :], sgate[:, j, :], ALU.mult), S["mixed"])

            def ada_make(l, c, half):
                n = ada_chunks[12 * l + c]
                slot = ring[:, n % RING, :].rearrange("p (k c) -> p k c", k=KT)
                if half == 0 and 12 * l + c >= 2:
                    turn.take(S["ada_raw"], conditions(l, c - 2) if c >= 2 else 1)
                if half == 0:
                    dve.wait_ge(slot_loaded[n % RING], 16 * (n // RING + 1))
                ws = range(conditions(l, c))
                for k in range(half * KT // 2, (half + 1) * KT // 2):
                    for w in ws:
                        to, by = made[:, c % 2, w, :], silu_c[:, k, w:w + 1]
                        if k:
                            turn.own(vchain, len(ws) - 1 - (w if k == KT - 1 else 0))
                            last = stt(to, slot[:, k, :], by, to, ALU.mult, ALU.add)
                        else:
                            last = V.tensor_scalar(to, slot[:, k, :], by, None, ALU.mult)
                        turn.give(last, S["ada_made"] if k == KT - 1 else vchain)

            def ffn(l):
                post_norm(gain("post_mix_g", l))
                pre_norm(gain("pre_ffn_g", l))
                for m in range(FT):
                    turn.take(S["ffn_sig"])
                    step(V.tensor_tensor(fft[:, m % 2, :], ps[:, next(gates), 0:T], sgt[:, m % 2, :], ALU.mult),
                         S["ffn_gate_read"])
                    step(V.tensor_tensor(ff[:, m, :], tile()[:, 0:T], fft[:, m % 2, :], ALU.mult), S["hidden"])
                    ada_make(l, m // 2, m % 2)
                for half in range(2):
                    ada_make(l, FT // 2, half)
                post_norm(gain("post_ffn_g", l))

            ffn(0)

            pre_norm(gain("pre_mix_g", 1))
            step(V.tensor_copy(gtok[:], tile()[:, 0:32].rearrange("p (a b) -> p a b", a=TT)), S["gates_tok"])
            step(V.tensor_copy(ghead[:, 0:2, :], tile()[0:8].rearrange("p (a b) -> p a b", a=2)), S["gates_head"])
            step(stt(ghead[:, 2, :], ghead[:, 1, :], -1.0, ghead[:, 1, :], ALU.mult, ALU.max), S["f_abs"])
            turn.take(S["f_ln"])
            step(stt(ghead[:, 1, :], ghead[:, 1, :], 0.0, ghead[:, 2, :], ALU.min, ALU.subtract))
            step(V.tensor_tensor_scan(ghead[:, 3, :], ghead[:, 1, :], zeros[0:8, 0:T], 0.0, ALU.add, ALU.add))
            step(V.tensor_tensor(ghead[:, 0, :], ghead[:, 0, :], ghead[:, 3, :], ALU.subtract), S["gate_a"])
            step(V.tensor_tensor_scan(ghead[:, 2, :], ghead[:, 0, :], ghead[:, 0, :], 0.0, ALU.max, ALU.max))
            step(V.tensor_tensor(ghead[:, 3, :], ghead[:, 3, :], ghead[:, 2, :], ALU.add), S["gate_m"])
            step(V.tensor_copy(acol[:], tile()[:, 0:16].rearrange("p (a b) -> p a b", a=TT)), S["acol_ready"])

            def exponents(n):
                big = tile()
                step(stt(darg[:, n % 2, 0:T], big[:, 0:T], acol[:, 0, n:n + 1], tri, ALU.subtract, ALU.max))
                step(stt(darg[:, n % 2, T:T + P], big[:, P:T], acol[:, 1, n:n + 1], tri[:, 0:P],
                         ALU.subtract, ALU.max), S["exponents"])
                return tile()

            scores = [exponents(0), exponents(1)]
            for n in range(HEADS):
                turn.take(S["decays"])
                step(V.tensor_tensor(pm[:, n % 2, :], scores[n][:, 0:384], dexp[:, n % 2, :], ALU.mult),
                     S["weighted"])
                if n + 2 < HEADS:
                    scores.append(exponents(n + 2))
                turn.take(S["absden"])
                step(V.tensor_tensor(tmp[:, 0, :], ps[:, 7, T:2 * T], absd[:, n % 2, :], ALU.max), S["den_read"])
                step(V.reciprocal(tmp[:, 1, :], tmp[:, 0, :]))
                step(V.tensor_tensor(y_m[:, n, :], tile()[:, 0:T], tmp[:, 1, :], ALU.mult), S["head_out"])
            turn.take(S["mo"], KT)
            for n in range(HEADS):
                turn.take(S["head_roots"])
                step(V.reciprocal(sq[:, n, :], sq[:, n, :]))
                step(stt(y_m[:, n, :], y_m[:, n, :], v("head_g")[:, n:n + 1], sq[:, n, :], ALU.mult, ALU.mult))
                step(V.tensor_tensor(y_m[:, n, :], y_m[:, n, :], so[:, n, :], ALU.mult), S["mixed"])
            ffn(1)

            turn.take(S["ada_raw"], 2)
            bias = v("b_ada").rearrange("p (l m) -> p l m", l=2)
            step(V.tensor_tensor(ada[:, :, :, 0], ada[:, :, :, 0], bias, ALU.add))
            step(V.tensor_tensor(ada[:, 0, 0:16, 1], ada[:, 0, 0:16, 1], bias[:, 0, 0:16], ALU.add))
            for i, (l, part, w, g) in enumerate(((0, 1, 0, "g_norm1"), (0, 1, 1, "g_norm1"), (0, 4, 0, "g_norm2"),
                                                 (1, 1, 0, "g_norm1"), (1, 4, 0, "g_norm2"))):
                step(stt(scale_g[:, i, :], ada[:, l, 8 * part:8 * part + 8, w], 1.0, gain(g, l), ALU.add, ALU.mult))

            def modulated_norm(dst, src, which, l, part, w, ready, from_root=root):
                inverse_root(from_root)
                for k in range(KT + 1):
                    if k < KT:
                        turn.give(stt(dst[:, k, :], src[:, k, :], scale_g[:, which, k:k + 1], rstd[:],
                                      ALU.mult, ALU.mult), vchain)
                    if k:
                        turn.own(vchain, k < KT)
                        turn.give(V.tensor_scalar(dst[:, k - 1, :], dst[:, k - 1, :],
                                                  ada[:, l, 8 * part + k - 1, w:w + 1], None, ALU.add), ready)
                turn.own(ready)

            modulated_norm(hc, ctxr, 1, 0, 0, 1, S["hc_ready"], root_c)
            modulated_norm(h, x, 0, 0, 0, 0, S["h_ready"])
            for kv in range(2):
                src = tile()
                step(V.tensor_tensor(rope_t[:, 0, :], src[:, 0:T], cos, ALU.mult))
                step(V.tensor_tensor(rope_t[:, 1, :], src[:, T:2 * T], sin, ALU.mult), S["k_rope_read"])
                step(V.tensor_tensor(kd[:, kv, T:2 * T], rope_t[:, 0, :], rope_t[:, 1, :], ALU.add))
            turn.take(S["qraw_ready"], HTL)
            for j in range(HTL):
                step(V.tensor_tensor(rope_t[:, 1, :], tile()[:, 0:T], sin, ALU.mult), S["q_rope_read"])
                step(V.tensor_tensor(rope_t[:, 0, :], q_a[:, j, :], cos, ALU.mult))
                step(V.tensor_tensor(q_a[:, j, :], rope_t[:, 0, :], rope_t[:, 1, :], ALU.add),
                     S["rotated"] if j == HTL - 1 else vchain)
            turn.take(S["z_gelu"], TT)
            for t in range(TT):
                step(V.tensor_reduce(small[:, 0:1], z_a[:, t, :], AX, ALU.add))
                step(V.tensor_scalar(small[:, 1:2], small[:, 0:1], 1.0 / HALF, None, ALU.mult))
                step(V.tensor_scalar(zc[:, t, :], z_a[:, t, :], small[:, 1:2], None, ALU.subtract),
                     S["z_centred"] if t == TT - 1 else vchain)
            turn.take(S["z_root"])
            turn.take(S["z_sq"], TT)
            turn.take(S["rows_spread"], 2)
            step(V.reciprocal(small[:, 8:10], small[:, 6:8]))
            for t in range(TT):
                step(stt(z_a[:, t, :], zc[:, t, :], small[:, 8 + t:9 + t], sgu_g[:], ALU.mult, ALU.mult),
                     S["z_normed"] if t == TT - 1 else vchain)

            def att_max(i):
                n, t, c = i // 2, i % 2, i % 2
                step(stt(sm[:, c, :], tile(), 0.125, window[:, t, :], ALU.mult, ALU.add), S["scores_read"])
                step(V.tensor_reduce(small[:, 16 + c:17 + c], sm[:, c, :], AX, ALU.max))
                step(V.tensor_scalar(small[:, 10 + c:11 + c], small[:, 16 + c:17 + c], sink[:, n:n + 1], -1.0,
                                     ALU.max, ALU.mult), S["maxima"])

            def att_probs(i):
                c = i % 2
                turn.take(S["exps"])
                step(V.tensor_tensor(small[:, 18 + c:19 + c], small[:, 12 + c:13 + c], small[:, 14 + c:15 + c],
                                     ALU.add))
                step(V.reciprocal(small[:, 18 + c:19 + c], small[:, 18 + c:19 + c]))
                step(V.tensor_scalar(pexp[:, c, :], pexp[:, c, :], small[:, 18 + c:19 + c], None, ALU.mult),
                     S["probs"])

            att_max(0)
            att_max(1)
            att_probs(0)
            for i in range(2 * HEADS):
                if i + 2 < 2 * HEADS:
                    att_max(i + 2)
                if i + 1 < 2 * HEADS:
                    att_probs(i + 1)
            turn.take(S["u_gelu"], HTL)
            for j in range(HTL):
                step(V.tensor_tensor(mix[:, HTL + j, :], tile()[:, 0:T], u_a[:, j, :], ALU.mult), S["mixed"])

            def add_to_x(src, k, l, part):
                step(stt(x[:, k, :], src, ada[:, l, 8 * part + k, 0:1], x[:, k, :], ALU.mult, ALU.add), S["x_added"])

            def one_hot(dst, values, top, n):
                step(V.tensor_scalar(rt[:, 0, 0:n], values, top, None, ALU.is_equal))
                step(V.tensor_tensor_scan(rt[:, 1, 0:n], rt[:, 0, 0:n], zeros[:, 0:n], 0.0, ALU.add, ALU.add))
                step(stt(dst, rt[:, 1, 0:n], 1.0, rt[:, 0, 0:n], ALU.is_equal, ALU.mult))

            def route(t):
                step(V.tensor_reduce(small[:, 24:25], lg[:, t, 0:NGRP], AX, ALU.max))
                step(V.tensor_scalar(small[:, 20:21], small[:, 24:25], -1.0, None, ALU.mult), S["router_max"])
                one_hot(small[:, 28:32], lg[:, t, 0:NGRP], small[:, 24:25], NGRP)
                step(V.tensor_scalar(small[:, 32:36], small[:, 28:32], 1.0, BIG, ALU.subtract, ALU.mult))
                for g in range(NGRP):
                    s = slice(NGRP + EPG * g, NGRP + EPG * (g + 1))
                    step(V.tensor_scalar(rt[:, 2, EPG * g:EPG * (g + 1)], lg[:, t, s], small[:, 32 + g:33 + g], None,
                                         ALU.add))
                step(V.tensor_reduce(small[:, 25:26], rt[:, 2, :], AX, ALU.max))
                one_hot(rt[:, 3, :], rt[:, 2, :], small[:, 25:26], NEXP)
                step(stt(rt[:, 2, :], rt[:, 3, :], -2.0 * BIG, rt[:, 2, :], ALU.mult, ALU.add))
                step(V.tensor_reduce(small[:, 26:27], rt[:, 2, :], AX, ALU.max))
                one_hot(rt[:, 4, :], rt[:, 2, :], small[:, 26:27], NEXP)
                turn.take(S["router_exp"])
                step(V.tensor_tensor(small[:, 22:23], small[:, 26:27], small[:, 25:26], ALU.subtract),
                     S["router_gap"])
                step(V.reciprocal(small[:, 36:37], small[:, 21:22]))
                turn.take(S["router_gexp"])
                step(V.tensor_scalar(small[:, 37:38], small[:, 23:24], 1.0, None, ALU.add))
                step(V.reciprocal(small[:, 38:39], small[:, 37:38]))
                step(V.tensor_tensor(small[:, 38:39], small[:, 38:39], small[:, 36:37], ALU.mult))
                step(V.tensor_tensor(small[:, 39:40], small[:, 38:39], small[:, 23:24], ALU.mult))
                step(V.tensor_scalar(G[:, t, 0:NEXP], rt[:, 3, :], small[:, 38:39], None, ALU.mult))
                step(stt(G[:, t, 0:NEXP], rt[:, 4, :], small[:, 39:40], G[:, t, 0:NEXP], ALU.mult, ALU.add))
                step(V.tensor_tensor(chosen[:, t, 0:NEXP], rt[:, 3, :], rt[:, 4, :], ALU.add),
                     S["chosen_ready"] if t == TT - 1 else vchain)

            def all_tokens(e_):
                V.memset(small[:, 50:51], 0.0).then_inc(e_["gate_freed"], 1)
                V.memset(small[:, 51:52], 0.0).then_inc(e_["gate_freed"], 1)
                V.memset(small[:, 52:53], 0.0).then_inc(e_["up_freed"], 1)
                V.memset(small[:, 53:54], 0.0).then_inc(e_["row_copied"], 1)
                with dve.Fori(0, NEXP // 2) as i:
                    for e in range(2):
                        dve.wait_ge(e_["row_copied"], 2 * i + e + 1)
                        V.tensor_scalar(dg[:, e, 0:P], ident, G[:, 0, bass.ds(2 * i + e, 1)], None, ALU.mult)
                        V.tensor_scalar(dg[:, e, P:T], ident, G[:, 1, bass.ds(2 * i + e, 1)], None,
                                        ALU.mult).then_inc(e_["diag"], 1)
                        for m in range(HTL):
                            dve.wait_ge(e_["gate_sig"], 8 * i + 4 * e + m + 1)
                            V.tensor_tensor(et[:, 0, :], ps[:, 2 * (m % 2), 0:T], esg[:, m % 2, :],
                                            ALU.mult).then_inc(e_["gate_freed"], 1)
                            dve.wait_ge(e_["gate_freed"], 8 * i + 4 * e + m + 3)
                            dve.wait_ge(e_["up_full"], 8 * i + 4 * e + m + 1)
                            V.tensor_tensor(et[:, 1, :], ps[:, 1, 0:T], et[:, 0, :], ALU.mult).then_inc(
                                e_["up_freed"], 1)
                            dve.wait_ge(e_["up_freed"], 8 * i + 4 * e + m + 2)
                            if m == 0:
                                dve.wait_ge(e_["row_copied"], 2 * i + e + 2)
                            V.tensor_tensor(hid[:, e, m * T:(m + 1) * T], et[:, 1, :], gb[:, e, :],
                                            ALU.mult).then_inc(e_["hid_ready"], 1)
                            dve.wait_ge(e_["hid_ready"], 8 * i + 4 * e + m + 1)

            def masks(e_, pair):
                for e in range(2):
                    for t in range(TT):
                        at, col = slice(e * CAP, (e + 1) * CAP), bass.ds(2 * pair + e, 1)
                        V.tensor_scalar(weigh[:, t, at], iota, place[:, t, col], G[:, t, col], ALU.is_equal, ALU.mult)
                        last = V.tensor_scalar(pick[:, t, at], iota, place[:, t, col], chosen[:, t, col],
                                               ALU.is_equal, ALU.mult)
                last.then_inc(e_["masks_ready"], 1)

            def gathered_tokens(e_):
                masks(e_, 0)
                with dve.Fori(0, NEXP // 2) as i:
                    dve.wait_ge(e_["weights_turned"], i + 1)
                    V.tensor_copy(spread, ps[:, 2, 0:T]).then_inc(e_["spread_ready"], 1)
                    masks(e_, i + 1)
                    dve.wait_ge(e_["gate_sig"], i + 1)
                    V.tensor_tensor(eg, ps[:, 0, :], sg, ALU.mult).then_inc(e_["gated"], 1)
                    dve.wait_ge(e_["gated"], i + 1)
                    dve.wait_ge(e_["gate_full"], 4 * i + 4)
                    V.tensor_tensor(hs, ps[:, 1, :], eg, ALU.mult).then_inc(e_["hid_ready"], 1)
                    dve.wait_ge(e_["hid_turned"], i + 1)
                    V.tensor_copy(hg, ps[:, 0, :]).then_inc(e_["hg_ready"], 1)

            def experts(l):
                e_ = E[l]
                modulated_norm(h, x, 2 if l == 0 else 4, l, 3, 0, S["h_ready"])
                step(V.tensor_copy(lg[:], tile()[:, 0:TT * NLOG].rearrange("p (a b) -> p a b", a=TT)),
                     S["logits_read"])
                for t in range(TT):
                    route(t)
                step(V.memset(G[:, :, NEXP:NE2], 0.0))
                step(V.memset(chosen[:, :, NEXP:NE2], 0.0))
                step(V.memset(place[:, :, NEXP:NE2], 0.0))
                counts = tile()
                step(V.tensor_copy(place[:, :, 0:NEXP], counts[:, 0:2 * NEXP].rearrange("p (a b) -> p a b", a=TT)))
                step(V.tensor_reduce(small[:, 27:28], counts[:, 2 * NEXP:3 * NEXP], AX, ALU.max))
                step(V.tensor_copy(crowd[:], small[:, 27:28]), S["crowd_ready"])
                most = dve.value_load(crowd[0:1, 0:1])
                with dve.If(most > CAP):
                    all_tokens(e_)
                with dve.Else():
                    gathered_tokens(e_)
                for b in range(4):
                    acc = tile()
                    for i in range(2):
                        add_to_x(acc[:, i * T:(i + 1) * T], 2 * b + i, l, 5)

            for k in range(KT):
                add_to_x(tile()[:, 0:T], k, 0, 2)
            experts(0)

            modulated_norm(h, x, 3, 1, 0, 0, S["h_ready"])
            step(V.memset(ypad[:, :, 0:1], 0.0))
            step(V.memset(ypad[:, :, T + 1:T + 2], 0.0))
            for k in range(KT):
                turn.take(S["cgate"])
                step(V.tensor_tensor(ypad[:, k, 1:T + 1], tile()[:, 0:T], cg[:, k, :], ALU.mult), S["cvalue"])
            cw = v("conv_w")
            for k in range(KT):
                step(V.tensor_scalar(cvo[:, k, :], ypad[:, k, 0:T], cw[:, 3 * k:3 * k + 1], None, ALU.mult))
                for i in (1, 2):
                    step(stt(cvo[:, k, :], ypad[:, k, i:i + T], cw[:, 3 * k + i:3 * k + i + 1], cvo[:, k, :],
                             ALU.mult, ALU.add))
            for k in range(KT):
                turn.take(S["bgate"])
                step(V.tensor_tensor(cvo[:, k, :], cvo[:, k, :], bg[:, k, :], ALU.mult), S["mixed"])
            for k in range(KT):
                add_to_x(tile()[:, 0:T], k, 1, 2)
            experts(1)
            pre_norm(v("g_final"))
            h_count.append(turn.given[S["h_ready"]])

        @block.sync
        def _(sp):
            sp.wait_ge(S["h_ready"], h_count[0])
            sp.dma_start(out, h[:]).then_inc(out_stored, 16)
            sp.wait_ge(out_stored, 16)


def tiled(w):
    import numpy as np
    k, n = w.shape
    w = w.reshape(k // P, P, n // CH, CH)
    return np.ascontiguousarray(w.transpose(2, 1, 0, 3))


def features(vector):
    import numpy as np
    vector = vector.reshape(-1, vector.shape[-1] // P, P)
    return np.ascontiguousarray(vector.transpose(2, 0, 1)).reshape(P, -1)


def shape_constants():
    import numpy as np
    f32 = np.float32
    con = np.zeros((P, NCON), f32)

    def put(name, value):
        con[:value.shape[0], CON[name][0]:CON[name][0] + CON[name][1]] = value.reshape(value.shape[0], -1)

    m, t = np.arange(P), np.arange(T)
    put("ident", np.eye(P, dtype=f32))
    inv = f32(10000.0) ** (-np.arange(16, dtype=f32) / f32(16))
    place = np.where((m % 64 < 32)[:, None], (t // 64)[None, :], (t % 64)[None, :]).astype(f32)
    angle = place * inv[m % 16][:, None]
    put("cos", np.cos(angle).astype(f32))
    put("sin", np.sin(angle).astype(f32))
    partner = np.zeros((P, P), f32)
    partner[np.where(m % 32 < 16, m + 16, m - 16), m] = np.where(m % 32 < 16, -1, 1)
    perm = [partner]
    for kv in range(2):
        both = np.zeros((P, P), f32)
        both[kv * 64 + m % 64, m] = 1
        perm.append(both)
    for kv in range(2):
        pair = np.zeros((P, P), f32)
        for c in range(P):
            pair[:, c] = perm[1 + kv][:, partner[:, c].nonzero()[0][0]] * partner[:, c].sum()
        perm.append(pair)
    put("perm", np.stack(perm, 1))
    put("tri", np.where(t[None, :] >= m[:, None], 0, BIG).astype(f32))
    key = np.arange(2 * T)[None, None, :] - T
    query = m[:, None, None] + P * np.arange(TT)[None, :, None]
    put("below", (m[:, None] < m[None, :]).astype(f32))
    put("iota", np.broadcast_to(np.arange(CAP, dtype=f32), (P, CAP)))
    put("window", np.where((key < 0) | (abs(key - query) <= P), 0, -BIG).astype(f32))
    eight = np.arange(8)
    sel8 = np.broadcast_to((eight[:, None] == eight[None, :])[:, :, None], (8, 8, P)).reshape(8, -1)
    selb = (eight[:, None, None] == 2 * np.arange(4)[None, :, None] + m[None, None, :] // 64).reshape(8, -1)
    return con, np.concatenate([sel8, selb], 1).astype(f32)


def kernel(**inputs):
    import numpy as np
    import concourse.bacc as bacc
    from concourse.bass_utils import run_bass_kernel_spmd as run

    g = {n: np.asarray(w) for n, w in inputs.items()}
    arrays = {}

    def feature_major(w):
        return np.ascontiguousarray(w.reshape(T, KT, P).transpose(2, 1, 0))

    arrays["x"] = feature_major(g["x"])
    arrays["ctx"] = feature_major(g["ctx_2"])
    arrays["ab_w_in"] = tiled(g["ab_w_in"][0])
    arrays["ab_w_out"] = tiled(g["ab_w_out"][0])
    arrays["ml_w_in"] = tiled(g["ml_w_in"][0][:, :3072])
    arrays["ml_w_out"] = tiled(g["ml_w_out"][0])

    def columns(w):
        pad = np.zeros((w.shape[0], 6 * CH), w.dtype)
        pad[:, :DFF] = w
        return tiled(pad)

    arrays["w_ff_gate"] = np.stack([columns(w) for w in g["ffn_w_gate"]])
    arrays["w_ff_up"] = np.stack([columns(w) for w in g["ffn_w_up"]])
    arrays["w_ff_down"] = np.stack([tiled(w) for w in g["ffn_w_down"]])
    arrays["w_ada"] = np.stack([tiled(w) for w in g["w_ada_2"]])
    even = g["w_in_even_2"][0]
    arrays["w_even"] = np.stack([tiled(even[:, c:c + CH])[0] for c in (0, 768, 1280)])
    arrays["w_even_kv"] = np.ascontiguousarray(even[:, 512:768].reshape(KT, P, 256).transpose(1, 0, 2))
    arrays["w_even_out"] = tiled(g["w_out_even_2"][0])
    arrays["w_odd"] = tiled(g["w_in_odd_2"][0])
    arrays["w_odd_out"] = tiled(g["w_out_odd_2"][0])
    for name in ("gate", "up"):
        w = g[f"w_{name}_2"].reshape(2, NEXP, KT, P, EH)
        arrays[f"w_{name}"] = np.ascontiguousarray(w.transpose(0, 1, 3, 2, 4)).reshape(2, NEXP, P, SLOT)
    w = g["w_down_2"].reshape(2, NEXP, HTL, P, D)
    arrays["w_down"] = np.ascontiguousarray(w.transpose(0, 1, 3, 2, 4)).reshape(2, NEXP, P, SLOT)

    mb = g["ml_b_in"][0]
    parts = dict(
        pre_mix_g=features(g["pre_mix_g"]), post_mix_g=features(g["post_mix_g"]),
        pre_ffn_g=features(g["pre_ffn_g"]), post_ffn_g=features(g["post_ffn_g"]),
        ab_b_in=features(g["ab_b_in"]),
        conf_w=np.ascontiguousarray(g["conf_conv_w"][0].reshape(CK, HTL, P).transpose(2, 1, 0)).reshape(P, -1),
        conf_b=features(g["conf_conv_b"]), ln_g=features(g["conf_ln_g"]), ln_b=features(g["conf_ln_b"]),
        lru_w=np.ascontiguousarray(g["lru_conv_w"][0].reshape(LK, HTL, P).transpose(2, 1, 0)).reshape(P, -1),
        lru_b=features(g["lru_conv_b"]), b_a=features(g["lru_b_a"].reshape(1, HALF)),
        b_x=features(g["lru_b_x"].reshape(1, HALF)), lam=features(g["lru_lambda"]),
        ml_b=features(np.concatenate([mb[0:1024], mb[2048:3072]])[None]), head_g=features(g["ml_head_g"]),
        c=np.ascontiguousarray(np.stack([g["c_2"][0], g["c_ctx_2"]]).reshape(2, KT, P).transpose(2, 1, 0)
                               ).reshape(P, -1),
        b_ada=features(g["b_ada_2"]), g_norm1=features(g["g_norm1_2"]), g_norm2=features(g["g_norm2_2"]),
        g_final=features(g["g_final_2"][None]),
        conv_w=np.ascontiguousarray(g["conv_w_2"][0].reshape(3, KT, P).transpose(2, 1, 0)).reshape(P, -1))
    arrays["vec"] = np.concatenate([parts[n] for n, _ in VEC_SIZES], 1)
    arrays["con"], arrays["sel"] = shape_constants()
    rows = dict(v_b=mb[1024:2048], gate_b=mb[3072:3088],
                router_b=np.concatenate([g["b_router_group_2"], g["b_router_expert_2"]], 1).reshape(-1),
                g_sgu=g["g_sgu_2"][0], sink=g["attn_sink_2"][0])
    arrays["row"] = np.concatenate([rows[n] for n, _ in ROW_SIZES])[None]
    arrays["gate_w"] = np.ascontiguousarray(g["ml_w_in"][0][:, 3072:].reshape(KT, P, 16).transpose(1, 0, 2))
    router = np.concatenate([g["w_router_group_2"], g["w_router_expert_2"]], 2)
    arrays["router_w"] = np.ascontiguousarray(router.reshape(2, KT, P, NLOG).transpose(2, 0, 1, 3))
    arrays["w_sp"] = np.ascontiguousarray(g["w_spatial_2"][0].transpose(2, 0, 1))
    arrays["b_sp"] = np.ascontiguousarray(g["b_spatial_2"][0])
    arrays["lru_w"] = np.ascontiguousarray(np.stack([g["lru_w_a"][0], g["lru_w_x"][0]]).reshape(
        2, HTL, 2, 64, 64).transpose(0, 2, 3, 1, 4))

    nc = bacc.Bacc("TRN2", target_bir_lowering=False, num_devices=1)
    handles = {n: nc.dram_tensor(f"in_{n}", w.shape, F32, kind="ExternalInput").ap() for n, w in arrays.items()}
    out = nc.dram_tensor("out", (P, KT, T), F32, kind="ExternalOutput").ap()
    build(nc, handles, out)
    result = run(nc, [{f"in_{n}": w for n, w in arrays.items()}], core_ids=[0])
    got = result.results[0]["out"]
    return np.ascontiguousarray(got.transpose(2, 1, 0).reshape(1, T, D))
```
